# Optimizing a Trainium2 kernel written in Bass

```python
import jax, jax.numpy as jnp
from jax import lax
import numpy as np

D_MODEL = 1024
BATCH = 1
SEQ = 128
DEPTH = 2
DEC_BATCH = 1
DEC_SEQ = 1024
PAST_LEN = 256

F32 = jnp.float32
GRID_W = 64
EPS = 1e-6
D_FF = 4 * D_MODEL
MIX_WIDTH = D_MODEL
N_EVEN = (DEPTH + 1) // 2
N_ODD = DEPTH // 2
N_DIR = 2

ATT_HEADS = 8
ATT_KV_HEADS = 2
HEAD_DIM = 64
ATT_WIDTH = ATT_HEADS * HEAD_DIM
ATT_KV_WIDTH = ATT_KV_HEADS * HEAD_DIM
ATT_GROUP = ATT_HEADS // ATT_KV_HEADS
ROPE_THETA = 10000.0
ROPE_PAIRS_PER_AXIS = HEAD_DIM // 4
Q_BLOCK = 128

MLSTM_HEADS = 4
MLSTM_HD = 128
MLSTM_WIDTH = MLSTM_HEADS * MLSTM_HD
MLSTM_CHUNK = 128
M_INIT = -1e30

LRU_WIDTH = 512
LRU_BLOCKS = 8
LRU_BD = LRU_WIDTH // LRU_BLOCKS
LRU_C = 8.0
CONV_W = 4
CONV_LEFT = 2

GLA_HEADS = 4
GLA_DK = 64
GLA_DV = 128
GLA_KW = GLA_HEADS * GLA_DK
GLA_WIDTH = GLA_HEADS * GLA_DV
GLA_RANK = 16
GLA_TAU = 16.0
GLA_CHUNK = 64

EVEN_SIZES = (ATT_WIDTH, ATT_KV_WIDTH, ATT_KV_WIDTH, MLSTM_WIDTH, MLSTM_WIDTH, MLSTM_WIDTH, MLSTM_WIDTH, N_DIR * MLSTM_HEADS, N_DIR * MLSTM_HEADS)
IN_EVEN = sum(EVEN_SIZES)
ODD_SIZES = (LRU_WIDTH, LRU_WIDTH, GLA_KW, GLA_KW, GLA_WIDTH, GLA_WIDTH, N_DIR * GLA_RANK)
IN_ODD = sum(ODD_SIZES)

kernel_name = 'hybrid_flow_trunk_step'

def split_cols(a, sizes):
    out, start = [], 0
    for s in sizes:
        out.append(a[..., start:start + s])
        start += s
    return out

def rms_norm(x, g):
    xf = x.astype(F32)
    y = xf * lax.rsqrt(jnp.mean(xf * xf, axis=-1, keepdims=True) + EPS)
    return (y * g.astype(F32)).astype(x.dtype)

def split_mod(mod):
    return jnp.split(mod[:, None, :], 6, axis=-1)

def modulate(x, g, shift, scale):
    return rms_norm(x, g) * (1 + scale) + shift

def gated_residual(x, y, g, gate):
    return x + gate * rms_norm(y, g)

def sq_relu_ffn(h, w1, w2):
    return jnp.square(jax.nn.relu(h @ w1)) @ w2

def flip(a):
    return jnp.flip(a, axis=1)

def axial_rope(n_tokens):
    rows = n_tokens // GRID_W
    row = jnp.repeat(jnp.arange(rows), GRID_W).astype(F32)
    col = jnp.tile(jnp.arange(GRID_W), rows).astype(F32)
    inv = jnp.power(ROPE_THETA, -jnp.arange(ROPE_PAIRS_PER_AXIS, dtype=F32) / ROPE_PAIRS_PER_AXIS)
    ang = jnp.concatenate([row[:, None] * inv, col[:, None] * inv], axis=-1)
    return jnp.cos(ang), jnp.sin(ang)

def apply_rope(x, cos, sin):
    x1, x2 = jnp.split(x, 2, axis=-1)
    c = cos[None, :, None, :].astype(x.dtype)
    s = sin[None, :, None, :].astype(x.dtype)
    return jnp.concatenate([x1 * c - x2 * s, x1 * s + x2 * c], axis=-1)

def block_attention(q, k, v):
    B, T, KV, G, HD = q.shape
    nb = T // Q_BLOCK
    qb = jnp.moveaxis(q.reshape(B, nb, Q_BLOCK, KV, G, HD), 1, 0)

    def one_block(qblk):
        s = jnp.einsum('bqkgd,bskd->bkgqs', qblk, k).astype(F32)
        p = jax.nn.softmax(s, axis=-1).astype(v.dtype)
        return jnp.einsum('bkgqs,bskd->bqkgd', p, v)

    o = lax.map(one_block, qb)
    return jnp.moveaxis(o, 0, 1).reshape(B, T, KV * G * HD)

def mlstm_scan(q, k, v, log_i, log_f, C0, n0, m0):
    B, T, H, D = q.shape
    L = MLSTM_CHUNK
    nc = T // L

    def chunk(a):
        return jnp.moveaxis(a.astype(F32).reshape((B, nc, L) + a.shape[2:]), 1, 0)

    causal = jnp.tril(jnp.ones((L, L), dtype=bool))[None, :, :, None]

    def step(carry, inp):
        C, n, m = carry
        qx, kx, vx, ix, fx = inp
        b = jnp.cumsum(fx, axis=1)
        g = b + m[:, None, :]
        dlog = jnp.where(causal, b[:, :, None] - b[:, None, :] + ix[:, None, :], -jnp.inf)
        m_t = jnp.maximum(g, jnp.max(dlog, axis=2))
        w = jnp.exp(dlog - m_t[:, :, None])
        w_inter = jnp.exp(g - m_t)
        qk = jnp.einsum('bthd,bshd->btsh', qx, kx) * w
        num = jnp.einsum('btsh,bshe->bthe', qk, vx) + w_inter[..., None] * jnp.einsum('bthd,bhde->bthe', qx, C)
        den = jnp.sum(qk, axis=2) + w_inter * jnp.einsum('bthd,bhd->bth', qx, n)
        h = num / jnp.maximum(jnp.abs(den), jnp.exp(-m_t))[..., None]
        b_last = b[:, -1]
        wlog = b_last[:, None] - b + ix
        m_new = jnp.maximum(b_last + m, jnp.max(wlog, axis=1))
        ws = jnp.exp(wlog - m_new[:, None])
        decay = jnp.exp(b_last + m - m_new)
        C_new = decay[..., None, None] * C + jnp.einsum('bsh,bshd,bshe->bhde', ws, kx, vx)
        n_new = decay[..., None] * n + jnp.einsum('bsh,bshd->bhd', ws, kx)
        return (C_new, n_new, m_new), h

    init = (C0.astype(F32), n0.astype(F32), m0.astype(F32))
    (C, n, m), h = lax.scan(step, init, (chunk(q), chunk(k), chunk(v), chunk(log_i), chunk(log_f)))
    return jnp.moveaxis(h, 0, 1).reshape(B, T, H, v.shape[-1]), (C, n, m)

def gla_scan(q, k, v, log_a, S0):
    B, T, H, DK = q.shape
    L = GLA_CHUNK
    nc = T // L

    def chunk(a):
        return jnp.moveaxis(a.astype(F32).reshape((B, nc, L) + a.shape[2:]), 1, 0)

    causal = jnp.tril(jnp.ones((L, L), dtype=bool))[None, :, :, None, None]

    def step(S, inp):
        qx, kx, vx, ax = inp
        b = jnp.cumsum(ax, axis=1)
        diff = b[:, :, None] - b[:, None, :]
        decay = jnp.where(causal, jnp.exp(jnp.minimum(diff, 0.0)), 0.0)
        scores = jnp.einsum('bthc,bshc,btshc->btsh', qx, kx, decay)
        o = jnp.einsum('btsh,bshe->bthe', scores, vx) + jnp.einsum('bthc,bhce->bthe', qx * jnp.exp(b), S)
        b_last = b[:, -1]
        S_new = jnp.exp(b_last)[..., None] * S + jnp.einsum('bshc,bshe->bhce', kx * jnp.exp(b_last[:, None] - b), vx)
        return S_new, o

    S_fin, o = lax.scan(step, S0.astype(F32), (chunk(q), chunk(k), chunk(v), chunk(log_a)))
    return jnp.moveaxis(o, 0, 1).reshape(B, T, H, v.shape[-1]), S_fin

def centred_depthwise_conv(x, w, b):
    T = x.shape[1]
    xp = jnp.pad(x, ((0, 0), (CONV_LEFT, CONV_W - 1 - CONV_LEFT), (0, 0)))
    y = b
    for j in range(CONV_W):
        y = y + xp[:, j:j + T] * w[j]
    return y

def _lin_combine(e1, e2):
    a1, b1 = e1
    a2, b2 = e2
    return a1 * a2, a2 * b1 + b2

def rglru(xc, w_r, b_r, w_i, b_i, lam, h0):
    B, T, W = xc.shape
    xb = xc.reshape(B, T, LRU_BLOCKS, LRU_BD)
    r = jax.nn.sigmoid(jnp.einsum('btnd,nde->btne', xb, w_r).reshape(B, T, W) + b_r)
    i = jax.nn.sigmoid(jnp.einsum('btnd,nde->btne', xb, w_i).reshape(B, T, W) + b_i)
    log_a = (-LRU_C * r.astype(F32)) * jax.nn.softplus(-lam.astype(F32))
    a = jnp.exp(log_a)
    u = jnp.sqrt(-jnp.expm1(2.0 * log_a)) * (i * xc).astype(F32)
    a_cum, h = lax.associative_scan(_lin_combine, (a, u), axis=1)
    h = h + a_cum * h0.astype(F32)[:, None]
    return h, h[:, -1]

def even_mixer(h, w_in, q_gain, k_gain, i_bias, f_bias, m_gain, rope, ctx_k, ctx_v, C0, n0, m0):
    B, T, _ = h.shape
    q, k, v, mq, mk, mv, mo, mi, mfg = split_cols(h @ w_in, EVEN_SIZES)
    q = rms_norm(q.reshape(B, T, ATT_HEADS, HEAD_DIM), q_gain)
    k = rms_norm(k.reshape(B, T, ATT_KV_HEADS, HEAD_DIM), k_gain)
    v = v.reshape(B, T, ATT_KV_HEADS, HEAD_DIM)
    if rope is None:
        k_all, v_all = k, v
    else:
        q = apply_rope(q, rope[0], rope[1])
        k = apply_rope(k, rope[0], rope[1])
        k_all = jnp.concatenate([jnp.swapaxes(ctx_k, 1, 2).astype(k.dtype), k], axis=1)
        v_all = jnp.concatenate([jnp.swapaxes(ctx_v, 1, 2).astype(v.dtype), v], axis=1)
    q = q.reshape(B, T, ATT_KV_HEADS, ATT_GROUP, HEAD_DIM) * HEAD_DIM ** -0.5
    attn = block_attention(q, k_all, v_all)
    mq = mq.reshape(B, T, MLSTM_HEADS, MLSTM_HD) * MLSTM_HD ** -0.5
    mk = mk.reshape(B, T, MLSTM_HEADS, MLSTM_HD)
    mv = mv.reshape(B, T, MLSTM_HEADS, MLSTM_HD)
    log_i = (mi.reshape(B, T, N_DIR, MLSTM_HEADS) + i_bias).astype(F32)
    log_f = jax.nn.log_sigmoid((mfg.reshape(B, T, N_DIR, MLSTM_HEADS) + f_bias).astype(F32))
    hf, (Cf, nf, mf_last) = mlstm_scan(mq, mk, mv, log_i[:, :, 0], log_f[:, :, 0], C0[:, 0], n0[:, 0], m0[:, 0])
    hb, (Cb, nb, mb_last) = mlstm_scan(flip(mq), flip(mk), flip(mv), flip(log_i[:, :, 1]), flip(log_f[:, :, 1]), C0[:, 1], n0[:, 1], m0[:, 1])
    hm = (hf + flip(hb)).astype(h.dtype)
    hm = rms_norm(hm, m_gain.reshape(MLSTM_HEADS, MLSTM_HD)).reshape(B, T, MLSTM_WIDTH) * jax.nn.sigmoid(mo)
    out = jnp.concatenate([attn, hm], axis=-1)
    ctx_state = (jnp.swapaxes(k, 1, 2), jnp.swapaxes(v, 1, 2), jnp.stack([Cf, Cb], axis=1), jnp.stack([nf, nb], axis=1), jnp.stack([mf_last, mb_last], axis=1))
    return out, ctx_state

def odd_mixer(h, w_in, conv_w, conv_b, w_r, b_r, w_i, b_i, lam, w_lr, b_lr, o_gain, h0, S0):
    B, T, _ = h.shape
    rx, rg, gq, gk, gv, gg, glr = split_cols(h @ w_in, ODD_SIZES)
    xc = centred_depthwise_conv(rx, conv_w, conv_b)
    hf, hf_last = rglru(xc, w_r[0], b_r[0], w_i[0], b_i[0], lam[0], h0[:, 0])
    hb, hb_last = rglru(flip(xc), w_r[1], b_r[1], w_i[1], b_i[1], lam[1], h0[:, 1])
    lru = jax.nn.gelu(rg) * (hf + flip(hb)).astype(h.dtype)
    gq = gq.reshape(B, T, GLA_HEADS, GLA_DK) * GLA_DK ** -0.5
    gk = gk.reshape(B, T, GLA_HEADS, GLA_DK)
    gv = gv.reshape(B, T, GLA_HEADS, GLA_DV)
    z = jnp.einsum('btrl,rlc->btrc', glr.reshape(B, T, N_DIR, GLA_RANK), w_lr) + b_lr
    log_a = (jax.nn.log_sigmoid(z.astype(F32)) / GLA_TAU).reshape(B, T, N_DIR, GLA_HEADS, GLA_DK)
    of, Sf = gla_scan(gq, gk, gv, log_a[:, :, 0], S0[:, 0])
    ob, Sb = gla_scan(flip(gq), flip(gk), flip(gv), flip(log_a[:, :, 1]), S0[:, 1])
    og = rms_norm((of + flip(ob)).astype(h.dtype), o_gain.reshape(GLA_HEADS, GLA_DV)).reshape(B, T, GLA_WIDTH) * jax.nn.silu(gg)
    out = jnp.concatenate([lru, og], axis=-1)
    ctx_state = (jnp.stack([hf_last, hb_last], axis=1), jnp.stack([Sf, Sb], axis=1))
    return out, ctx_state

def setup_inputs(seed: int = 0) -> dict:
    key = jax.random.key(seed)
    keys = iter(jax.random.split(key, 48))

    def nrm(shape, scale=1.0):
        return scale * jax.random.normal(next(keys), shape, F32)

    def gain(shape):
        return 1.0 + 0.05 * jax.random.normal(next(keys), shape, F32)

    lam_a = jax.random.uniform(next(keys), (N_ODD, N_DIR, LRU_WIDTH), F32, 0.9, 0.999)
    lam_s = lam_a ** (1.0 / LRU_C)
    f_bias = 3.0 + 3.0 * jax.random.uniform(next(keys), (N_EVEN, N_DIR, MLSTM_HEADS), F32)
    return {
        'x_prompt': nrm((BATCH, SEQ, D_MODEL)),
        'x_sample': nrm((DEC_BATCH, DEC_SEQ, D_MODEL)),
        'cache_attn_k': nrm((DEC_BATCH, N_EVEN, ATT_KV_HEADS, PAST_LEN, HEAD_DIM)),
        'cache_attn_v': nrm((DEC_BATCH, N_EVEN, ATT_KV_HEADS, PAST_LEN, HEAD_DIM)),
        'state_mlstm_C': nrm((DEC_BATCH, N_EVEN, N_DIR, MLSTM_HEADS, MLSTM_HD, MLSTM_HD), 0.5),
        'state_mlstm_n': nrm((DEC_BATCH, N_EVEN, N_DIR, MLSTM_HEADS, MLSTM_HD), 0.5),
        'state_mlstm_m': nrm((DEC_BATCH, N_EVEN, N_DIR, MLSTM_HEADS)),
        'state_lru_h': nrm((DEC_BATCH, N_ODD, N_DIR, LRU_WIDTH), 0.5),
        'state_gla_S': nrm((DEC_BATCH, N_ODD, N_DIR, GLA_HEADS, GLA_DK, GLA_DV), 0.5),
        'c': nrm((DEC_BATCH, D_MODEL)),
        'c_ctx': nrm((D_MODEL,)),
        'ada_w': nrm((DEPTH, D_MODEL, 6 * D_MODEL), D_MODEL ** -0.5),
        'ada_b': nrm((DEPTH, 6 * D_MODEL), 0.02),
        'norm_mix_pre': gain((DEPTH, D_MODEL)),
        'norm_mix_post': gain((DEPTH, D_MODEL)),
        'norm_ffn_pre': gain((DEPTH, D_MODEL)),
        'norm_ffn_post': gain((DEPTH, D_MODEL)),
        'w_out': nrm((DEPTH, MIX_WIDTH, D_MODEL), MIX_WIDTH ** -0.5),
        'ffn_w1': nrm((DEPTH, D_MODEL, D_FF), D_MODEL ** -0.5),
        'ffn_w2': nrm((DEPTH, D_FF, D_MODEL), D_FF ** -0.5),
        'w_in_even': nrm((N_EVEN, D_MODEL, IN_EVEN), D_MODEL ** -0.5),
        'attn_q_norm': gain((N_EVEN, HEAD_DIM)),
        'attn_k_norm': gain((N_EVEN, HEAD_DIM)),
        'mlstm_i_bias': nrm((N_EVEN, N_DIR, MLSTM_HEADS), 0.1),
        'mlstm_f_bias': f_bias,
        'mlstm_norm': gain((N_EVEN, MLSTM_WIDTH)),
        'w_in_odd': nrm((N_ODD, D_MODEL, IN_ODD), D_MODEL ** -0.5),
        'lru_conv_w': nrm((N_ODD, CONV_W, LRU_WIDTH), CONV_W ** -0.5),
        'lru_conv_b': nrm((N_ODD, LRU_WIDTH), 0.02),
        'lru_w_r': nrm((N_ODD, N_DIR, LRU_BLOCKS, LRU_BD, LRU_BD), LRU_BD ** -0.5),
        'lru_b_r': nrm((N_ODD, N_DIR, LRU_WIDTH), 0.1),
        'lru_w_i': nrm((N_ODD, N_DIR, LRU_BLOCKS, LRU_BD, LRU_BD), LRU_BD ** -0.5),
        'lru_b_i': nrm((N_ODD, N_DIR, LRU_WIDTH), 0.1),
        'lru_lambda': jnp.log(lam_s) - jnp.log1p(-lam_s),
        'gla_w_lr': nrm((N_ODD, N_DIR, GLA_RANK, GLA_KW), GLA_RANK ** -0.5),
        'gla_b_lr': nrm((N_ODD, N_DIR, GLA_KW), 0.1),
        'gla_norm': gain((N_ODD, GLA_WIDTH)),
    }

def reference(x_prompt, x_sample, cache_attn_k, cache_attn_v, state_mlstm_C, state_mlstm_n, state_mlstm_m, state_lru_h, state_gla_S, c, c_ctx, ada_w, ada_b, norm_mix_pre, norm_mix_post, norm_ffn_pre, norm_ffn_post, w_out, ffn_w1, ffn_w2, w_in_even, attn_q_norm, attn_k_norm, mlstm_i_bias, mlstm_f_bias, mlstm_norm, w_in_odd, lru_conv_w, lru_conv_b, lru_w_r, lru_b_r, lru_w_i, lru_b_i, lru_lambda, gla_w_lr, gla_b_lr, gla_norm):
    rope = axial_rope(x_sample.shape[1])
    silu_ctx = jax.nn.silu(c_ctx)[None]
    silu_c = jax.nn.silu(c)
    Bp = x_prompt.shape[0]
    zC = jnp.zeros((Bp, N_DIR, MLSTM_HEADS, MLSTM_HD, MLSTM_HD), F32)
    zn = jnp.zeros((Bp, N_DIR, MLSTM_HEADS, MLSTM_HD), F32)
    zm = jnp.full((Bp, N_DIR, MLSTM_HEADS), M_INIT, F32)
    zh = jnp.zeros((Bp, N_DIR, LRU_WIDTH), F32)
    zS = jnp.zeros((Bp, N_DIR, GLA_HEADS, GLA_DK, GLA_DV), F32)
    xp, xs = x_prompt, x_sample
    ks, vs, Cs, ns, ms, hs_, Ss = [], [], [], [], [], [], []
    for l in range(DEPTH):
        sh_ap, sc_ap, gt_ap, sh_mp, sc_mp, gt_mp = split_mod(silu_ctx @ ada_w[l] + ada_b[l])
        sh_as, sc_as, gt_as, sh_ms, sc_ms, gt_ms = split_mod(silu_c @ ada_w[l] + ada_b[l])
        hp = modulate(xp, norm_mix_pre[l], sh_ap, sc_ap)
        hs = modulate(xs, norm_mix_pre[l], sh_as, sc_as)
        if l % 2 == 0:
            e = l // 2
            yp, (k_c, v_c, C_c, n_c, m_c) = even_mixer(hp, w_in_even[e], attn_q_norm[e], attn_k_norm[e], mlstm_i_bias[e], mlstm_f_bias[e], mlstm_norm[e], None, None, None, zC, zn, zm)
            ys, _ = even_mixer(hs, w_in_even[e], attn_q_norm[e], attn_k_norm[e], mlstm_i_bias[e], mlstm_f_bias[e], mlstm_norm[e], rope, cache_attn_k[:, e], cache_attn_v[:, e], state_mlstm_C[:, e], state_mlstm_n[:, e], state_mlstm_m[:, e])
            ks.append(k_c)
            vs.append(v_c)
            Cs.append(C_c)
            ns.append(n_c)
            ms.append(m_c)
        else:
            o = l // 2
            yp, (h_c, S_c) = odd_mixer(hp, w_in_odd[o], lru_conv_w[o], lru_conv_b[o], lru_w_r[o], lru_b_r[o], lru_w_i[o], lru_b_i[o], lru_lambda[o], gla_w_lr[o], gla_b_lr[o], gla_norm[o], zh, zS)
            ys, _ = odd_mixer(hs, w_in_odd[o], lru_conv_w[o], lru_conv_b[o], lru_w_r[o], lru_b_r[o], lru_w_i[o], lru_b_i[o], lru_lambda[o], gla_w_lr[o], gla_b_lr[o], gla_norm[o], state_lru_h[:, o], state_gla_S[:, o])
            hs_.append(h_c)
            Ss.append(S_c)
        xp = gated_residual(xp, yp @ w_out[l], norm_mix_post[l], gt_ap)
        xs = gated_residual(xs, ys @ w_out[l], norm_mix_post[l], gt_as)
        xp = gated_residual(xp, sq_relu_ffn(modulate(xp, norm_ffn_pre[l], sh_mp, sc_mp), ffn_w1[l], ffn_w2[l]), norm_ffn_post[l], gt_mp)
        xs = gated_residual(xs, sq_relu_ffn(modulate(xs, norm_ffn_pre[l], sh_ms, sc_ms), ffn_w1[l], ffn_w2[l]), norm_ffn_post[l], gt_ms)
    dt = x_prompt.dtype
    y_prompt = xp
    y_sample = xs
    new_attn_k = jnp.stack(ks, axis=1).astype(dt)
    new_attn_v = jnp.stack(vs, axis=1).astype(dt)
    new_mlstm_C = jnp.stack(Cs, axis=1).astype(dt)
    new_mlstm_n = jnp.stack(ns, axis=1).astype(dt)
    new_mlstm_m = jnp.stack(ms, axis=1).astype(dt)
    new_lru_h = jnp.stack(hs_, axis=1).astype(dt)
    new_gla_S = jnp.stack(Ss, axis=1).astype(dt)
    return (y_prompt, y_sample, new_attn_k, new_attn_v, new_mlstm_C, new_mlstm_n, new_mlstm_m, new_lru_h, new_gla_S)


_drawn_inputs = setup_inputs


def setup_inputs(seed=0):
    import zlib

    import numpy as np

    out = dict(_drawn_inputs(seed))
    spreads = {}
    factors = {'cache_attn_k': 4.246,
     'cache_attn_v': 3.381,
     'state_mlstm_C': 11.789,
     'state_mlstm_n': 77.437,
     'state_mlstm_m': 4.71,
     'state_lru_h': 18.621,
     'state_gla_S': 8.0,
     'attn_q_norm': 8.0,
     'mlstm_norm': 2.834,
     'lru_b_r': 4.522,
     'gla_norm': 62.998}
    for name, (base, spread) in spreads.items():
        noise = np.random.default_rng([zlib.crc32(name.encode()), seed]).standard_normal(out[name].shape)
        drawn = base * np.exp(spread * noise) if base else spread * noise
        out[name] = __import__('jax').numpy.asarray(drawn.astype(out[name].dtype))
    for name, factor in factors.items():
        out[name] = (out[name] * factor).astype(out[name].dtype)
    return out
```

```python
from contextlib import ExitStack

import numpy as np
import concourse.bass as bass
from concourse import mybir

F32 = mybir.dt.float32
F32R = mybir.dt.float32r
ALU = mybir.AluOpType
ACT = mybir.ActivationFunctionType
AX = mybir.AxisListType
ds = bass.ds

P = 128
D = 1024
KD = D // P
SAMPLE_TILES, TILES = 8, 9
T = TILES * P
CTX = 8
LAYERS = 2
FF = 4 * D
EPS = 1e-6
NEG = -1e30

HEADS, KV, HD = 8, 2, 64
PAST = 256
MH, MD = 4, 128
GH, GK, GV = 4, 64, 128
RANK = 16
LW = 512

EVEN_GROUPS = [(0, 512, "T"), (512, 272, "T"), (784, 512, "F"), (1296, 512, "T"), (1808, 512, "T"), (2320, 512, "T")]
ODD_GROUPS = [(0, 512, "F"), (512, 512, "F"), (1024, 512, "F"), (1536, 512, "T"), (2048, 512, "T"), (2560, 32, "F")]
GROUPS = [EVEN_GROUPS, ODD_GROUPS]
N_GROUPS = 6
FG = 256
NG = FF // FG
TB = 384


class Chain:

    def __init__(self, eng, sem):
        self.eng, self.sem, self.base, self.k, self.i, self.per = eng, sem, 0, 0, 0, 0

    def loop(self, i, per):
        self.base, self.k, self.i, self.per = self.base + self.k, 0, i, per

    def end(self, n):
        assert self.k == self.per, (self.k, self.per)
        self.base, self.k, self.i, self.per = self.base + n * self.per, 0, 0, 0

    def mark(self, ins):
        self.k += 1
        ins.then_inc(self.sem, 1)

    def sync(self):
        self.eng.wait_ge(self.sem, self.i * self.per + (self.base + self.k))

    def link(self, ins):
        self.mark(ins)
        self.sync()


def trunk(nc, A):
    st = ExitStack()
    with st:
        slab = st.enter_context(nc.sbuf_tensor("slab", [P, 212800 // 4], F32))
        K = 1024
        SBUF0 = 16512
        CONST, AT0, WT0, RAW0, SCR0, END = 0, 14 * K, 86 * K, 154 * K, 170 * K, 170 * K + 38 * K - 230

        class Region:

            def __init__(self, start, end):
                self.at, self.end = start, end

            def __call__(self, name, shape, dt=F32):
                n = 4 * int(np.prod(shape[1:]))
                t = nc.alloc_sbuf_tensor_at(name, shape, dt, offset=SBUF0 + self.at)
                self.at += (n + 31) // 32 * 32
                assert self.at <= self.end, (name, self.at, self.end)
                return t

        sem = lambda name: st.enter_context(nc.semaphore(name))
        STAGE_SEMS = 38
        stage_set = [sem(f"stage{n}") for n in range(STAGE_SEMS)]

        class Stage:
            def __init__(self):
                self.names = {}

            def __call__(self, name):
                self.names[name] = stage_set[len(self.names)]
                return self.names[name]

        psum = st.enter_context(nc.psum_tensor("psum", [P, 8, 512], F32))

        const = Region(CONST, AT0)
        ident = const("ident", [P, P])
        ones = const("ones", [P, P])
        modc = const("modc", [P, LAYERS, 48, 2])
        ada_bias = const("ada_bias", [P, LAYERS, 48, 2])
        gains = const("gains", [P, LAYERS, 4, KD, 2])
        pre_scale = const("pre_scale", [P, LAYERS, 2, KD, 2])
        post_scale = const("post_scale", [P, LAYERS, 2, KD, 2])
        silu_c = const("silu_c", [P, KD, 2])
        silu_t = const("silu_t", [P, KD, 2])
        eps = const("eps", [P, 1])
        stats = const("stats", [P, 32])
        gate_row_at = (const.at + 31) // 32 * 32
        gate_row = const("gate_row", [P, 2, D])
        relu_t = Region(gate_row_at, AT0)("relu_t", [P, 3, TB])

        AT = Region(AT0, WT0)("AT", [P, 2, KD, T], F32R)
        WT = Region(WT0, RAW0)("WT", [P, 2, 2, 4096], F32R)
        WF = Region(WT0, RAW0)("WF", [P, 2, 2, 2048], F32R)
        H1 = Region(WT0 + 32 * K, RAW0)("H1", [P, 2, 2, 2, T], F32R)
        RAW = Region(RAW0, SCR0)("RAW", [P, 4096])
        ada_raws = [Region(WT0, RAW0)("ada_raw0", [P, 2, 4096]), Region(SCR0, END)("ada_raw1", [P, 2, 4096])]

        ada_acc = Region(gate_row_at, AT0)("ada_acc", [P, 2, 2, 512])
        ada_scaled = Region(SCR0 + 32 * K, END)("ada_scaled", [P, 2, 512])

        ATf = AT[:].bitcast(F32)
        WTf = WT[:].bitcast(F32)
        WFf = WF[:].bitcast(F32)
        H1f = H1[:].bitcast(F32)

        const_in = sem("const_in")
        const_ready = sem("const_ready")
        silu_step = sem("silu_step")
        silu_ready = sem("silu_ready")
        ada_in = [sem(f"ada_in{s}") for s in range(2)]
        ada_part = sem("ada_part")
        ada_begun = sem("ada_begun")
        ada_scaled_ready = [sem(f"ada_scaled_ready{n}") for n in range(2)]
        ada_added = [sem(f"ada_added{n}") for n in range(2)]
        ada_sum = [sem(f"ada_sum{s}") for s in range(2)]
        ada_kept = [sem(f"ada_kept{s}") for s in range(2)]
        phase_done = sem("phase_done")
        N_CONST_LOADS = 3
        dchain_sem = sem("dve_chain")
        achain_sem = sem("act_chain")
        phases = {}

        def barrier(eng, name):
            n = phases.setdefault(name, len(phases) + 1)
            eng.drain().then_inc(phase_done, 1)
            eng.wait_ge(phase_done, 5 * n)

        def next_stage(eng, name, clear=False):
            barrier(eng, name)
            if clear:
                for s in stage_set:
                    nc.gpsimd.sem_clear(s)
            barrier(eng, name + ", cleared")
            eng.drain()

        ada_v = [A["ada_w"][l].rearrange("(k p) n -> p k n", p=P) for l in range(LAYERS)]

        def const_sync(sp):
            sp.dma_start(silu_c[:, :, :], A["c_cols"]).then_inc(const_in, 16)
            sp.dma_start(ada_bias[:, :, :, :], A["ada_b"]).then_inc(const_in, 16)
            sp.dma_start(gains[:, :, :, :, :], A["gains"]).then_inc(const_in, 16)

        def const_gpsimd(pool):
            nc.gpsimd.memset(ones[:, :], 1.0).then_inc(const_ready, 1)
            nc.gpsimd.memset(eps[:, :], EPS).then_inc(const_ready, 1)
            nc.gpsimd.memset(ident[:, :], 0.0).then_inc(const_ready, 1)
            pool.wait_ge(const_ready, 3)
            nc.gpsimd.affine_select(out=ident[:, :], in_=ident[:, :], compare_op=ALU.not_equal, fill=1.0,
                                    base=0, pattern=[[-1, P]], channel_multiplier=1).then_inc(const_ready, 1)

        def silu_scalar(act):
            act.wait_ge(const_in, 16 * N_CONST_LOADS)
            nc.scalar.activation(silu_t[:, :, :], silu_c[:, :, :], ACT.Exp, scale=-1.0).then_inc(silu_step, 1)

        def silu_vector(dve, chain):
            dve.wait_ge(silu_step, 1)
            chain.link(nc.vector.tensor_scalar(silu_t[:, :, :], silu_t[:, :, :], 1.0, None, ALU.add))
            chain.link(nc.vector.reciprocal(silu_t[:, :, :], silu_t[:, :, :]))
            nc.vector.tensor_tensor(silu_c[:, :, :], silu_c[:, :, :], silu_t[:, :, :], ALU.mult).then_inc(silu_ready, 1)

        def ada_load(sp, l, s, j):
            sp.wait_ge(ada_sum[s], j + 6 * l)
            sp.dma_start(ada_raws[l][:, s, :].rearrange("p (k n) -> p k n", k=KD), ada_v[l][:, :, ds(j * 1024 + 512 * s, 512)]).then_inc(ada_in[s], 16)

        def ada_sync(sp):
            with sp.Fori(0, 6) as j:
                for s in range(2):
                    ada_load(sp, 0, s, j)

        def ada_latent(dve, l, s, j):
            acc = ada_acc[:, s, 0, :]
            dve.wait_ge(ada_in[s], 16 * j + (16 * (6 * l + 1)))
            dve.wait_ge(ada_sum[s], j + 6 * l)
            for k in range(KD):
                w, c = ada_raws[l][:, s, k * 512:(k + 1) * 512], silu_c[:, k, 0:1]
                if k:
                    dve.wait_ge(ada_part, j * 16 + (96 * l + 8 * s + k))
                    nc.vector.scalar_tensor_tensor(acc, w, c, acc, ALU.mult, ALU.add).then_inc(ada_part, 1)
                else:
                    nc.vector.tensor_scalar(acc, w, c, None, ALU.mult).then_inc(ada_part, 1)

        def ada_uses(l, s, j, k):
            n = (3, 4)[k % 2]
            return j * (2 * n) + ((12 * l + s) * n + (k - 1) // 2)

        def ada_scalar(act, l, s, j):
            act.wait_ge(ada_in[s], 16 * j + (16 * (6 * l + 1)))
            act.wait_ge(ada_sum[s], j + 6 * l)
            for k in range(KD):
                w, c = ada_raws[l][:, s, k * 512:(k + 1) * 512], silu_c[:, k, 1:2]
                if k:
                    act.wait_ge(ada_added[k % 2], ada_uses(l, s, j, k))
                    nc.scalar.activation(ada_scaled[:, k % 2, :], w, ACT.Copy, scale=c).then_inc(ada_scaled_ready[k % 2], 1)
                else:
                    nc.scalar.activation(ada_acc[:, s, 1, :], w, ACT.Copy, scale=c).then_inc(ada_begun, 1)

        def ada_gpsimd(pool, l, s, j):
            acc = ada_acc[:, s, 1, :]
            for k in range(1, KD):
                pool.wait_ge(ada_scaled_ready[k % 2], ada_uses(l, s, j, k) + 1)
                if k == 1:
                    pool.wait_ge(ada_begun, j * 2 + (12 * l + s + 1))
                else:
                    pool.wait_ge(ada_added[1 - k % 2], ada_uses(l, s, j, k - 1) + 1)
                nc.gpsimd.tensor_tensor(acc, acc, ada_scaled[:, k % 2, :], ALU.add).then_inc(ada_added[k % 2], 1)

        def ada_products(pe, l, s, j, bank):
            pe.wait_ge(ada_kept[s], j + 6 * l)
            for who in range(2):
                if who:
                    pe.wait_ge(ada_added[1], ada_uses(l, s, j, 7) + 1)
                else:
                    pe.wait_ge(ada_part, j * 16 + (96 * l + 8 * s + KD))
                for m in range(4):
                    at = 256 + 8 * s + 2 * m + who
                    mm = nc.tensor.matmul(psum[:, bank, at:at + 1], ada_acc[:, s, who, m * P:(m + 1) * P], ones[:, 0:1], start=True, stop=True)
            mm.then_inc(ada_sum[s], 1)

        def ada_keep(dve, l, s, j, bank):
            dve.wait_ge(ada_sum[s], j + (6 * l + 1))
            at = j * 16 + (8 * s + 96 * l)
            nc.vector.tensor_tensor(modc[:].rearrange("p l n s -> p (l n s)")[:, ds(at, 8)], psum[:, bank, 256 + 8 * s:256 + 8 * s + 8],
                                    ada_bias[:].rearrange("p l n s -> p (l n s)")[:, ds(at, 8)], ALU.add).then_inc(ada_kept[s], 1)

        def ada_scales(dve, chain, l):
            for s in range(2):
                dve.wait_ge(ada_kept[s], 6 * (l + 1))
            for sub in range(2):
                scale = modc[:, l, 24 * sub + 8:24 * sub + 16, :]
                gate = modc[:, l, 24 * sub + 16:24 * sub + 24, :]
                chain.mark(nc.vector.scalar_tensor_tensor(pre_scale[:, l, sub, :, :], scale, 1.0, gains[:, l, 2 * sub, :, :], ALU.add, ALU.mult))
                chain.link(nc.vector.tensor_tensor(post_scale[:, l, sub, :, :], gate, gains[:, l, 2 * sub + 1, :, :], ALU.mult))

        def ada_tensor(pe):
            with pe.Fori(0, 6) as j:
                for s in range(2):
                    ada_products(pe, 0, s, j, s)

        def ada_vector(dve, chain):
            dve.wait_ge(silu_ready, 1)
            with dve.Fori(0, 6) as j:
                for s in range(2):
                    ada_latent(dve, 0, s, j)
                    ada_keep(dve, 0, s, j, s)
            ada_scales(dve, chain, 0)

        class NormBuffers:
            def __init__(self, tag, region):
                self.x = [region(f"{tag}_x{s}", [P, D]) for s in range(2)]
                self.n = [region(f"{tag}_n{s}", [P, D]) for s in range(2)]
                self.v = region(f"{tag}_v", [P, KD, P])
                self.junk = region(f"{tag}_junk", [P, D])

        norm_mix = NormBuffers("mix", Region(SCR0, END))
        norm_ffn = NormBuffers("ffn", Region(WT0 + 32 * K, RAW0))
        x_in = [sem(f"x_in{s}") for s in range(2)]
        x_out = [sem(f"x_out{s}") for s in range(2)]
        x_new = [sem(f"x_new{s}") for s in range(2)]
        x_gone = [sem(f"x_gone{s}") for s in range(2)]
        inv_ready = [sem(f"inv_ready{s}") for s in range(2)]
        normed = [sem(f"normed{s}") for s in range(2)]
        turned = [sem(f"turned{s}") for s in range(2)]
        v_ready = [sem(f"v_ready{s}") for s in range(2)]
        at_high = [sem(f"at_high{s}") for s in range(2)]
        at_low = [sem(f"at_low{s}") for s in range(2)]
        PASSES = [(0, 0), (0, 1), (1, 0)]

        def ssq_scalar(act, chain, src, junk, s, out):
            chain.link(nc.scalar.activation(junk, src, ACT.Square, accum_out=stats[:, 4 * s:4 * s + 1]))
            chain.link(nc.scalar.activation(stats[:, 4 * s + 1:4 * s + 2], stats[:, 4 * s:4 * s + 1], ACT.Ln, bias=eps[:, :], scale=1.0 / D))
            return nc.scalar.activation(out, stats[:, 4 * s + 1:4 * s + 2], ACT.Exp, scale=-0.5)

        def tile_cols(i):
            return ds(i * P, P)

        def rows(t, tile):
            return t[ds(tile, 1)].rearrange("a p n -> (a p) n")

        def staged(eng, first, second, chain=None, per=0):
            first(0, 0, 0, 0)
            with eng.Fori(0, 3) as j:
                if chain:
                    chain.loop(j, per)
                first(j * 2 + 1, 1, j, 0)
                second(j * 2, 0, j, 0)
                first(j * 2 + 2, 0, j + 1, 0)
                second(j * 2 + 1, 1, j, 0)
            if chain:
                chain.end(3)
            first(7, 1, 3, 0)
            second(6, 0, 3, 0)
            first(CTX, 0, 4, 1)
            second(7, 1, 3, 0)
            second(CTX, 0, 4, 1)

        x_all = A["x_all"]
        xs = [x_all, nc.dram_tensor("x_1", [TILES, P, D], F32, kind="Internal").ap(), nc.dram_tensor("x_2", [TILES, P, D], F32, kind="Internal").ap(),
              nc.dram_tensor("x_3", [TILES, P, D], F32, kind="Internal").ap(), A["y_all"]]
        y_sum = [sem(f"y_sum{s}") for s in range(2)]
        y_inv = [sem(f"y_inv{s}") for s in range(2)]
        yacc = Region(SCR0, END)("yacc", [P, TILES, D])

        def pass_of(q):
            l, sub = (0, 0) if q == 0 else (q // 2, q % 2)
            return norm_mix if q in (0, 1, 3) else norm_ffn, (5 * q, 4 * q), l, sub

        def y_of(q, s, tile):
            if q in (1, 3):
                return psum[:, 2 * s:2 * s + 2, :].rearrange("p b n -> p (b n)")
            return yacc[:, ds(tile, 1), :].rearrange("p a n -> p (a n)")

        def pass_sync(sp, q):
            B, base, l, sub = pass_of(q)
            if q in (1, 3):
                load_group(sp, 4 * q + 3)

            def load(tile, s, j, who):
                gone = j * 16 + 16 * (base[s] - (5, 4)[s])
                if q and not isinstance(j, int):
                    gone = sp.compute_val(gone)
                if q < 4:
                    sp.wait_ge(normed[s], j + base[s])
                if q:
                    sp.wait_ge(x_gone[s], gone)
                sp.dma_start(B.x[s][:, :], rows(xs[max(q - 1, 0)], tile)).then_inc(x_in[s], 16)

            def store(tile, s, j, who):
                if q:
                    sp.wait_ge(x_new[s], j + (base[s] - (5, 4)[s] + 1))
                    sp.dma_start(rows(xs[q], tile), B.x[s][:, :]).then_inc(x_gone[s], 16)
            staged(sp, load, store)
            for s in range(2):
                if q:
                    sp.wait_ge(x_gone[s], 16 * (5, 4)[s] * q)

        def pass_scalar(act, chain, q):
            nc.scalar.preload_act_table_set("natural_log_exp_and_others")
            B, base, l, sub = pass_of(q)
            if q in (1, 3):
                split_high(act, 4 * q + 3)

            def first(tile, s, j, who):
                if q:
                    if q in (1, 3):
                        act.wait_ge(y_sum[s], j + ((5, 4)[s] * (q // 2) + 1))
                    act.wait_ge(x_new[s], j + (base[s] - (5, 4)[s]))
                    ssq_scalar(act, chain, y_of(q, s, tile), B.junk[:, :], 2 + s, stats[:, 4 * s + 10:4 * s + 11]).then_inc(y_inv[s], 1)
                    act.wait_ge(x_new[s], j + (base[s] - (5, 4)[s] + 1))
                else:
                    act.wait_ge(x_in[s], 16 * j + 16)
                if q < 4:
                    act.wait_ge(normed[s], j + base[s])
                    ssq_scalar(act, chain, B.x[s][:, :], B.junk[:, :], s, stats[:, 4 * s + 2:4 * s + 3]).then_inc(inv_ready[s], 1)

            def second(tile, s, j, who):
                if q < 4:
                    act.wait_ge(v_ready[s], j + (base[s] + 1))
                    nc.scalar.activation(AT[:, 0, :, tile_cols(tile)], B.v[:, :, :], ACT.Copy).then_inc(at_high[s], 1)
            staged(act, first, second, chain, 4 * (1 if q == 0 else 2 if q < 4 else 1))

        def pass_vector(dve, chain, q):
            B, base, l, sub = pass_of(q)

            def first(tile, s, j, who):
                if q:
                    dve.wait_ge(y_inv[s], j + (base[s] - (5, 4)[s] + 1))
                    dve.wait_ge(x_in[s], 16 * j + (16 * base[s] + 16))
                    chain.link(nc.vector.scalar_tensor_tensor(B.n[s][:, :], y_of(q, s, tile), stats[:, 4 * s + 10:4 * s + 11], gate_row[:, who, :],
                                                              ALU.mult, ALU.mult))
                    nc.vector.tensor_tensor(B.x[s][:, :], B.x[s][:, :], B.n[s][:, :], ALU.add).then_inc(x_new[s], 1)
                if q < 4:
                    dve.wait_ge(inv_ready[s], j + (base[s] + 1))
                    nc.vector.tensor_scalar(B.n[s][:, :], B.x[s][:, :], stats[:, 4 * s + 2:4 * s + 3], None, ALU.mult).then_inc(normed[s], 1)

            def second(tile, s, j, who):
                if q < 4:
                    dve.wait_ge(turned[s], j + (base[s] + 1))
                    dve.wait_ge(at_low[1 - s], j + (base[1 - s] + s))
                    for k in range(KD):
                        ins = nc.vector.tensor_scalar(B.v[:, k, :], psum[:, 6 + k // 4, (k % 4) * P:(k % 4 + 1) * P],
                                                      pre_scale[:, l, sub, k, who:who + 1], modc[:, l, 24 * sub + k, who:who + 1], ALU.mult, ALU.add)
                    ins.then_inc(v_ready[s], 1)
            staged(dve, first, second, chain, 2 if q else 0)

        def pass_tensor(pe, q):
            B, base, l, sub = pass_of(q)

            def first(tile, s, j, who):
                if q not in (1, 3):
                    return
                pe.wait_ge(x_new[s], j + (base[s] - (5, 4)[s]))
                for h in range(2):
                    g = 8 * (q // 2) + N_GROUPS + h
                    for k in range(KD):
                        for n, (a, b) in enumerate(PASSES):
                            mm = nc.tensor.matmul(psum[:, 2 * s + h, :], AT[:, a, k, tile_cols(tile)], wt(g, b, 512)[:, k, :],
                                                  start=(k == 0 and n == 0), stop=(k == KD - 1 and n == 2))
                mm.then_inc(y_sum[s], 1)

            def second(tile, s, j, who):
                if q == 4:
                    return
                pe.wait_ge(normed[s], j + (base[s] + 1))
                pe.wait_ge(v_ready[1 - s], j + (base[1 - s] + s))
                for k in range(KD):
                    mm = nc.tensor.transpose(psum[:, 6 + k // 4, (k % 4) * P:(k % 4 + 1) * P], B.n[s][:, k * P:(k + 1) * P], ident[:, :])
                mm.then_inc(turned[s], 1)
            if q in (1, 3):
                pe.wait_ge(w_low, 8 * (q // 2) + 8)
                first(0, 0, 0, 0)
                for t in range(TILES):
                    if t + 1 < TILES:
                        first(t + 1, (t + 1) % 2, (t + 1) // 2, 0)
                    second(t, t % 2, t // 2, 0)
            else:
                staged(pe, first, second)

        def pass_gpsimd(pool, q):
            B, base, l, sub = pass_of(q)
            if q in (1, 3):
                split_low(pool, 4 * q + 3)

            def second(tile, s, j, who):
                pool.wait_ge(at_high[s], j + (base[s] + 1))
                nc.gpsimd.tensor_tensor(AT[:, 1, :, tile_cols(tile)], B.v[:, :, :], ATf[:, 0, :, tile_cols(tile)], ALU.subtract).then_inc(at_low[s], 1)
            if q < 4:
                staged(pool, lambda *a: None, second)

        diag_mix = Region(SCR0 + 24 * K, END)("diag_mix", [P, 4, P])
        diag_ffn = Region(WT0 + 56 * K, RAW0)("diag_ffn", [P, 4, P])
        diag_ready = sem("diag_ready")
        row_sum = sem("row_sum")
        row_kept = sem("row_kept")

        def gate_vector(dve, l, sub):
            diag = (diag_mix, diag_ffn)[sub]
            for u in range(4):
                n = 4 * (2 * l + sub) + u
                if u:
                    dve.wait_ge(row_sum, n)
                for k in range(4):
                    ins = nc.vector.tensor_scalar(diag[:, k, :], ident[:, :], post_scale[:, l, sub, 4 * (u % 2) + k, u // 2:u // 2 + 1], None, ALU.mult)
                ins.then_inc(diag_ready, 1)

        def gate_tensor(pe, l, sub):
            diag = (diag_mix, diag_ffn)[sub]
            for u in range(4):
                n = 4 * (2 * l + sub) + u
                pe.wait_ge(diag_ready, n + 1)
                pe.wait_ge(row_kept, n)
                nc.tensor.matmul(psum[:, 5, :], ones[:, :], diag[:].rearrange("p k n -> p (k n)"), start=True, stop=True).then_inc(row_sum, 1)

        def gate_scalar(act, l, sub):
            for u in range(4):
                n = 4 * (2 * l + sub) + u
                act.wait_ge(row_sum, n + 1)
                nc.scalar.activation(gate_row[:, u // 2, (u % 2) * 512:(u % 2 + 1) * 512], psum[:, 5, :], ACT.Copy).then_inc(row_kept, 1)

        w_in = sem("w_in")
        w_high = sem("w_high")
        w_low = sem("w_low")

        def group_source(g):
            l, c = g // 8, g % 8
            if c < N_GROUPS:
                c0, width, _ = GROUPS[l][c]
                return A["w_in_even" if l == 0 else "w_in_odd"].rearrange("(k p) n -> p k n", p=P)[:, :, c0:c0 + width], width
            return A["w_out"][l].rearrange("(k p) n -> p k n", p=P)[:, :, (c - N_GROUPS) * 512:(c - N_GROUPS + 1) * 512], 512

        def wt(g, hl, width):
            return WT[:, g % 2, hl, 0:KD * width].rearrange("p (k n) -> p k n", k=KD)

        def group_done(g):
            l, c = g // 8, g % 8
            if c < N_GROUPS:
                return proj_sum[2], uses_before(l, c) + group_shape(l, c)[1]
            return y_sum[0], 5 * (l + 1)

        def load_group(sp, g):
            src, width = group_source(g)
            if g:
                sp.wait_ge(w_low, g)
            sp.dma_start(RAW[:, 0:KD * width].rearrange("p (k n) -> p k n", k=KD), src).then_inc(w_in, 16)

        def split_high(act, g):
            n = KD * group_source(g)[1]
            act.wait_ge(w_in, 16 * (g + 1))
            if g >= 2:
                act.wait_ge(*group_done(g - 2))
            nc.scalar.activation(WT[:, g % 2, 0, 0:n], RAW[:, 0:n], ACT.Copy).then_inc(w_high, 1)

        def split_low(pool, g):
            n = KD * group_source(g)[1]
            pool.wait_ge(w_high, g + 1)
            if g >= 2:
                pool.wait_ge(*group_done(g - 2))
            nc.gpsimd.tensor_tensor(WT[:, g % 2, 1, 0:n], RAW[:, 0:n], WTf[:, g % 2, 0, 0:n], ALU.subtract).then_inc(w_low, 1)

        proj_sum = [sem(f"proj_sum{s}") for s in range(3)]
        proj_kept = [sem(f"proj_kept{s}") for s in range(3)]
        proj_out = [sem(f"proj_out{s}") for s in range(3)]
        stage = [Region(at, end)(f"stage{n}", [P, 512]) for n, (at, end) in enumerate(
            ((WT0 + 64 * K, RAW0), (WT0 + 66 * K, RAW0), (gate_row_at + 8 * K, AT0)))]
        feat = [nc.dram_tensor("feat_even", [TILES, P, 2832], F32, kind="Internal").ap(),
                nc.dram_tensor("feat_odd", [TILES, P, 2592], F32, kind="Internal").ap()]
        featT = [nc.dram_tensor("featT_even", [4, P, T], F32, kind="Internal").ap(),
                 nc.dram_tensor("featT_odd", [13, P, T], F32, kind="Internal").ap()]
        FIRST_F = [{2: 0}, {0: 0, 1: 4, 2: 8, 5: 12}]

        def group_shape(l, c):
            _, width, kind = GROUPS[l][c]
            if kind == "T":
                return kind, 3, P
            return kind, max(1, width // P), min(P, width)

        def uses_before(l, c):
            return sum(group_shape(ll, cc)[1] for ll in range(LAYERS) for cc in range(N_GROUPS) if (ll, cc) < (l, c))

        def ada_slots(l):
            return range(2 if l == 0 else 0)

        def proj_tensor(pe, l):
            for c in range(N_GROUPS):
                kind, iters, feats = group_shape(l, c)
                g, width, base = 8 * l + c, GROUPS[l][c][1], uses_before(l, c)
                pe.wait_ge(w_low, g + 1)
                for i in range(iters):
                    for s in range(3):
                        pe.wait_ge(proj_kept[s], i + base)
                        for k in range(KD):
                            for n, (a, b) in enumerate(PASSES):
                                first, last = k == 0 and n == 0, k == KD - 1 and n == 2
                                if kind == "T":
                                    mm = nc.tensor.matmul(psum[:, s, 0:width], AT[:, a, k, ds(i * TB + s * P, P)], wt(g, b, width)[:, k, :],
                                                          start=first, stop=last)
                                else:
                                    mm = nc.tensor.matmul(psum[0:feats, s, 0:TB], wt(g, a, width)[:, k, ds(i * P, feats)] if iters > 1 else wt(g, a, width)[:, k, 0:feats],
                                                          AT[:, b, k, s * TB:(s + 1) * TB], start=first, stop=last)
                        mm.then_inc(proj_sum[s], 1)
                    if i == 0 and c:
                        for s in ada_slots(l):
                            ada_products(pe, 1, s, c - 1, 6 + s)
            for s in ada_slots(l):
                ada_products(pe, 1, s, N_GROUPS - 1, 6 + s)

        def proj_vector(dve, chain):
            for c in range(N_GROUPS):
                for s in range(2):
                    ada_latent(dve, 1, s, c)
                    ada_keep(dve, 1, s, c, 6 + s)
            ada_scales(dve, chain, 1)

        def proj_scalar(act, l):
            for c in range(N_GROUPS):
                kind, iters, feats = group_shape(l, c)
                g, width, base = 8 * l + c, GROUPS[l][c][1], uses_before(l, c)
                if c == 0:
                    split_high(act, g)
                split_high(act, g + 1)
                scale = MD ** -0.5 if (l, c) == (0, 2) else 1.0

                def evacuate(i):
                    for s in range(3):
                        act.wait_ge(proj_sum[s], i + (base + 1))
                        act.wait_ge(proj_out[s], 16 * i + 16 * base)
                        w = width if kind == "T" else TB
                        nc.scalar.activation(stage[s][0:feats, 0:w], psum[0:feats, s, 0:w], ACT.Copy, scale=scale).then_inc(proj_kept[s], 1)

                with act.Fori(0, iters - len(ada_slots(l)) // 2) as i:
                    evacuate(i)
                for s in ada_slots(l):
                    if s:
                        evacuate(iters - 1)
                    ada_scalar(act, 1, s, c)

        def proj_gpsimd(pool, l):
            for c in range(N_GROUPS):
                if c == 0:
                    split_low(pool, 8 * l)
                split_low(pool, 8 * l + c + 1)
                for s in ada_slots(l):
                    ada_gpsimd(pool, 1, s, c)

        def proj_sync(sp, l):
            for c in range(N_GROUPS):
                kind, iters, feats = group_shape(l, c)
                g, (c0, width, _), base = 8 * l + c, GROUPS[l][c], uses_before(l, c)
                if c == 0:
                    load_group(sp, g)
                    load_group(sp, g + 1)
                    for s in ada_slots(l):
                        ada_load(sp, 1, s, 0)
                if c + 2 < 7:
                    load_group(sp, g + 2)
                with sp.Fori(0, iters) as i:
                    for s in range(3):
                        sp.wait_ge(proj_kept[s], i + (base + 1))
                        if kind == "T":
                            sp.dma_start(feat[l][ds(i * 3 + s, 1), :, c0:c0 + width].rearrange("a p n -> (a p) n"), stage[s][:, 0:width]).then_inc(proj_out[s], 16)
                        else:
                            sp.dma_start(featT[l][ds(i + FIRST_F[l][c], 1), 0:feats, s * TB:(s + 1) * TB].rearrange("a p n -> (a p) n"),
                                         stage[s][0:feats, 0:TB]).then_inc(proj_out[s], 16)
                for s in ada_slots(l) if c + 1 < N_GROUPS else ():
                    ada_load(sp, 1, s, c + 1)
            for s in range(3):
                sp.wait_ge(proj_out[s], 16 * uses_before(l, N_GROUPS))

        w1_in, w1_high, w1_low = sem("w1_in"), sem("w1_high"), sem("w1_low")
        w2_in, w2_high, w2_low = sem("w2_in"), sem("w2_high"), sem("w2_low")
        up_sum = [sem(f"up_sum{s}") for s in range(3)]
        relu_ready = [sem(f"relu_ready{s}") for s in range(3)]
        square_ready = [sem(f"square_ready{s}") for s in range(3)]
        h_high = [sem(f"h_high{s}") for s in range(3)]
        h_low = [sem(f"h_low{s}") for s in range(3)]
        down_sum = [sem(f"down_sum{s}") for s in range(3)]
        down_kept = [sem(f"down_kept{s}") for s in range(3)]
        yacc_clear = sem("yacc_clear")
        w1_raw = RAW[:, 0:2048]
        w2_raw = RAW[:, 2048:4096]
        w1_part = [WF[:, 0, hl, :].rearrange("p (k n) -> p k n", k=KD) for hl in range(2)]
        w2_part = [WF[:, 1, hl, :].rearrange("p (m n) -> p m n", m=2) for hl in range(2)]

        def mlp_sync(sp, l):
            w1_v = A["ffn_w1"][l].rearrange("(k p) n -> p k n", p=P)
            w2_v = A["ffn_w2"][l].rearrange("(m p) n -> p m n", p=P)
            with sp.Fori(0, NG) as g:
                sp.wait_ge(w1_low, g + NG * l)
                sp.dma_start(w1_raw.rearrange("p (k n) -> p k n", k=KD), w1_v[:, :, ds(g * FG, FG)]).then_inc(w1_in, 16)
                sp.wait_ge(w2_low, g + NG * l)
                sp.dma_start(w2_raw.rearrange("p (m n) -> p m n", m=2), w2_v[:, ds(g * 2, 2), :]).then_inc(w2_in, 16)

        def pipelined(eng, up, down, chain=None, per=0):
            up(0, 0)
            with eng.Fori(0, NG // 2 - 1) as j:
                if chain:
                    chain.loop(j, per)
                up(j * 2 + 1, 1)
                down(j * 2, 0)
                up(j * 2 + 2, 0)
                down(j * 2 + 1, 1)
            if chain:
                chain.end(NG // 2 - 1)
            up(NG - 1, 1)
            down(NG - 2, 0)
            down(NG - 1, 1)

        def mlp_tensor(pe, l):
            def up(g, slot):
                pe.wait_ge(w1_low, g + (NG * l + 1))
                for m in range(2):
                    for tb in range(3):
                        pe.wait_ge(relu_ready[tb], g * 2 + (2 * NG * l + m))
                        for k in range(KD):
                            for n, (a, b) in enumerate(PASSES):
                                mm = nc.tensor.matmul(psum[:, tb, 0:TB], w1_part[a][:, k, m * P:(m + 1) * P], AT[:, b, k, tb * TB:(tb + 1) * TB],
                                                      start=(k == 0 and n == 0), stop=(k == KD - 1 and n == 2))
                        mm.then_inc(up_sum[tb], 1)

            def down(g, slot):
                pe.wait_ge(w2_low, g + (NG * l + 1))
                for tb in range(3):
                    pe.wait_ge(h_low[tb], g * 2 + (2 * NG * l + 2))
                for i in range(3):
                    for u in range(6):
                        bank = u % 3
                        pe.wait_ge(down_kept[bank], g * 6 + i * 2 + (6 * NG * l + u // 3))
                        for m in range(2):
                            for n, (a, b) in enumerate(PASSES):
                                mm = nc.tensor.matmul(psum[:, 3 + bank, :], H1[:, slot, a, m, ds(i * TB + (u // 2) * P, P)],
                                                      w2_part[b][:, m, (u % 2) * 512:(u % 2 + 1) * 512],
                                                      start=(m == 0 and n == 0), stop=(m == 1 and n == 2))
                        mm.then_inc(down_sum[bank], 1)
            pipelined(pe, up, down)

        def mlp_scalar(act, l):
            def w1_split(g):
                act.wait_ge(w1_in, g * 16 + 16 * (NG * l + 1))
                act.wait_ge(up_sum[2], g * 2 + 2 * NG * l)
                nc.scalar.activation(WF[:, 0, 0, :], w1_raw, ACT.Copy).then_inc(w1_high, 1)

            def w2_split(g):
                act.wait_ge(w2_in, g * 16 + 16 * (NG * l + 1))
                act.wait_ge(down_sum[2], g * 6 + 6 * NG * l)
                nc.scalar.activation(WF[:, 1, 0, :], w2_raw, ACT.Copy).then_inc(w2_high, 1)

            def up(g, slot):
                for m in range(2):
                    for tb in range(3):
                        act.wait_ge(up_sum[tb], g * 2 + (2 * NG * l + m + 1))
                        act.wait_ge(h_low[tb], g * 2 + (2 * NG * l + m))
                        nc.scalar.activation(relu_t[:, tb, :], psum[:, tb, 0:TB], ACT.Relu).then_inc(relu_ready[tb], 1)
                    if m == 0 and not (isinstance(g, int) and g == 0):
                        act.wait_ge(down_sum[2], g * 6 + (6 * NG * l - 6))
                    for tb in range(3):
                        act.wait_ge(square_ready[tb], g * 2 + (2 * NG * l + m + 1))
                        nc.scalar.activation(H1[:, slot, 0, m, tb * TB:(tb + 1) * TB], relu_t[:, tb, :], ACT.Copy).then_inc(h_high[tb], 1)

            w1_split(0)
            w2_split(0)
            pipelined_splits(act, up, w1_split, w2_split)

        def pipelined_splits(eng, up, w1_split, w2_split):
            up(0, 0)
            w1_split(1)
            with eng.Fori(0, NG // 2 - 1) as j:
                up(j * 2 + 1, 1)
                w1_split(j * 2 + 2)
                w2_split(j * 2 + 1)
                up(j * 2 + 2, 0)
                w1_split(j * 2 + 3)
                w2_split(j * 2 + 2)
            up(NG - 1, 1)
            w2_split(NG - 1)

        def mlp_vector(dve, l):
            nc.vector.memset(yacc[:, :, :], 0.0).then_inc(yacc_clear, 1)

            def up(g, slot):
                for m in range(2):
                    for tb in range(3):
                        dve.wait_ge(relu_ready[tb], g * 2 + (2 * NG * l + m + 1))
                        nc.vector.tensor_tensor(relu_t[:, tb, :], relu_t[:, tb, :], relu_t[:, tb, :], ALU.mult).then_inc(square_ready[tb], 1)

            def down(g, slot):
                kept = g * 6 + 6 * NG * l
                if not isinstance(g, int):
                    kept = dve.compute_val(kept)
                dve.wait_ge(yacc_clear, l + 1)
                for bank in range(3):
                    dve.wait_ge(down_kept[bank], kept)
                with dve.Fori(0, 3) as i:
                    for u in range(6):
                        bank = u % 3
                        dve.wait_ge(down_sum[bank], g * 6 + i * 2 + (6 * NG * l + u // 3 + 1))
                        y = yacc[:, ds(i * 3 + u // 2, 1), (u % 2) * 512:(u % 2 + 1) * 512].rearrange("p a n -> p (a n)")
                        nc.vector.tensor_tensor(y, y, psum[:, 3 + bank, :], ALU.add).then_inc(down_kept[bank], 1)
            pipelined(dve, up, down)

        def mlp_gpsimd(pool, l):
            def w1_split(g):
                pool.wait_ge(w1_high, g + (NG * l + 1))
                nc.gpsimd.tensor_tensor(WF[:, 0, 1, :], w1_raw, WFf[:, 0, 0, :], ALU.subtract).then_inc(w1_low, 1)

            def w2_split(g):
                pool.wait_ge(w2_high, g + (NG * l + 1))
                nc.gpsimd.tensor_tensor(WF[:, 1, 1, :], w2_raw, WFf[:, 1, 0, :], ALU.subtract).then_inc(w2_low, 1)

            def up(g, slot):
                for m in range(2):
                    for tb in range(3):
                        pool.wait_ge(h_high[tb], g * 2 + (2 * NG * l + m + 1))
                        nc.gpsimd.tensor_tensor(H1[:, slot, 1, m, tb * TB:(tb + 1) * TB], relu_t[:, tb, :], H1f[:, slot, 0, m, tb * TB:(tb + 1) * TB],
                                                ALU.subtract).then_inc(h_low[tb], 1)
            w1_split(0)
            w2_split(0)
            pipelined_splits(pool, up, w1_split, w2_split)

        KEYS = PAST + SAMPLE_TILES * P
        KT = KEYS // P
        att = Region(RAW0, END)
        kT = att("kT", [P, KEYS + P])
        qT = att("qT", [P, 4, T])
        vK = att("vK", [P, KT + 1, P])
        att_shared = att.at
        prob = att("prob", [P, 2, KEYS])
        probT = att("probT", [P, 2, KEYS])
        att_out = att("att_out", [P, 2, 512])
        q_now = Region(gate_row_at, AT0)("q_now", [P, 4, P])
        pre = Region(att_shared, END)
        qk_x = pre("qk_x", [P, 2, 10, HD])
        qk_sq = pre("qk_sq", [P, 10, HD])
        qk_cos = pre("qk_cos", [P, 10, 2, 32])
        qk_sin = pre("qk_sin", [P, 10, 2, 32])
        qk_rot = pre("qk_rot", [P, 2, 10, 2, 32])
        rope_t = pre("rope_t", [P, 2, 2, 32])
        qk_gain = pre("qk_gain", [P, 10, HD])
        qk_inv = pre("qk_inv", [P, 2, 10])
        sem_of = Stage()
        qk_const_in = sem_of("qk_const_in")
        qk_in = [sem_of(f"qk_in{s}") for s in range(2)]
        qk_ssq = [sem_of(f"qk_ssq{s}") for s in range(2)]
        qk_inv_ready = [sem_of(f"qk_inv_ready{s}") for s in range(2)]
        qk_rotated = [sem_of(f"qk_rotated{s}") for s in range(2)]
        qk_turned = [sem_of(f"qk_turned{s}") for s in range(2)]
        qk_kept = [sem_of(f"qk_kept{s}") for s in range(2)]
        kv_out = sem_of("kv_out")

        def pairs(eng, body, chain=None, per=0):
            with eng.Fori(0, 4) as j:
                if chain:
                    chain.loop(j, per)
                for s in range(2):
                    body(j * 2 + s, s, j)
            if chain:
                chain.end(4)
            body(CTX, 0, 4)

        def qk_sync(sp):
            sp.dma_start(qk_gain[:].rearrange("p h d -> p (h d)"), A["qk_gain"].to_broadcast([P, 10 * HD])).then_inc(qk_const_in, 16)
            sp.dma_start(kT[:, 0:PAST], A["cache_kT"]).then_inc(qk_const_in, 16)
            sp.dma_start(vK[:, 0:2, :], A["cache_v"]).then_inc(qk_const_in, 16)
            sp.dma_start(vK[:, 2:KT + 1, :], feat[0][:, :, 640:768].rearrange("t p n -> p t n")).then_inc(qk_const_in, 16)

            def body(tile, s, j):
                sp.wait_ge(qk_rotated[s], j)
                sp.dma_start(qk_x[:, s, :, :].rearrange("p h d -> p (h d)"), rows(feat[0], tile)[:, 0:640]).then_inc(qk_in[s], 16)
                sp.dma_start(rope_t[:, s, :, :], A["rope"][ds(tile, 1)].rearrange("a p c n -> (a p) c n")).then_inc(qk_in[s], 16)
            pairs(sp, body)
            sp.wait_ge(qk_const_in, 64)
            sp.dma_start(A["new_v"], vK[:, KT, :]).then_inc(kv_out, 16)
            sp.wait_ge(qk_rotated[0], 5)
            sp.dma_start(A["new_k"], qk_rot[:, 0, 8:10, :, :].rearrange("p h c n -> p (h c n)")).then_inc(kv_out, 16)
            sp.wait_ge(kv_out, 32)

        def qk_vector(dve, chain):
            dve.wait_ge(qk_const_in, 64)

            def body(tile, s, j):
                dve.wait_ge(qk_in[s], 32 * j + 32)
                x = qk_x[:, s, :, :]
                chain.link(nc.vector.tensor_tensor(qk_sq[:, :, :], x, x, ALU.mult))
                dve.wait_ge(qk_inv_ready[s], j)
                nc.vector.tensor_reduce(qk_inv[:, s, :], qk_sq[:, :, :], AX.X, ALU.add).then_inc(qk_ssq[s], 1)
                dve.wait_ge(qk_inv_ready[s], j + 1)
                chain.link(nc.vector.tensor_tensor(x, x, qk_inv[:, s, :].unsqueeze(2).to_broadcast([P, 10, HD]), ALU.mult))
                chain.link(nc.vector.tensor_tensor(x, x, qk_gain[:, :, :], ALU.mult))
                xh = x.rearrange("p h (c n) -> p (h c) n", c=2)
                chain.mark(nc.vector.tensor_tensor(qk_cos[:].rearrange("p h c n -> p (h c) n"), xh, rope_t[:, s, 0:1, :].to_broadcast([P, 20, 32]), ALU.mult))
                chain.link(nc.vector.tensor_tensor(qk_sin[:].rearrange("p h c n -> p (h c) n"), xh, rope_t[:, s, 1:2, :].to_broadcast([P, 20, 32]), ALU.mult))
                dve.wait_ge(qk_turned[s], j)
                chain.mark(nc.vector.tensor_tensor(qk_rot[:, s, :, 0, :], qk_cos[:, :, 0, :], qk_sin[:, :, 1, :], ALU.subtract))
                nc.vector.tensor_tensor(qk_rot[:, s, :, 1, :], qk_sin[:, :, 0, :], qk_cos[:, :, 1, :], ALU.add).then_inc(qk_rotated[s], 1)
            pairs(dve, body, chain, 12)

        def qk_scalar(act, chain):
            nc.scalar.preload_act_table_set("natural_log_exp_and_others")
            def body(tile, s, j):
                act.wait_ge(qk_ssq[s], j + 1)
                chain.link(nc.scalar.activation(qk_inv[:, s, :], qk_inv[:, s, :], ACT.Ln, bias=eps[:, :], scale=1.0 / HD))
                nc.scalar.activation(qk_inv[:, s, :], qk_inv[:, s, :], ACT.Exp, scale=-0.5).then_inc(qk_inv_ready[s], 1)
                act.wait_ge(qk_turned[s], j + 1)
                nc.scalar.activation(qT[:, :, tile_cols(tile)], psum[:, 2 * s, :].rearrange("p (j n) -> p j n", j=4), ACT.Copy, scale=HD ** -0.5)
                nc.scalar.activation(kT[:, ds(tile * P + PAST, P)], psum[:, 2 * s + 1, 0:P], ACT.Copy).then_inc(qk_kept[s], 1)
            pairs(act, body, chain, 2)

        def qk_tensor(pe):
            def body(tile, s, j):
                pe.wait_ge(qk_rotated[s], j + 1)
                pe.wait_ge(qk_kept[s], j)
                flat = qk_rot[:, s, :, :, :].rearrange("p h c n -> p (h c n)")
                for b in range(5):
                    mm = nc.tensor.transpose(psum[:, 2 * s + b // 4, (b % 4) * P:(b % 4 + 1) * P], flat[:, b * P:(b + 1) * P], ident[:, :])
                mm.then_inc(qk_turned[s], 1)
            pairs(pe, body)

        sem_of = Stage()
        score_done = [sem_of(f"score_done{s}") for s in range(2)]
        max_done = [sem_of(f"max_done{s}") for s in range(2)]
        prob_done = [sem_of(f"prob_done{s}") for s in range(2)]
        turn_done = [sem_of(f"turn_done{c}") for c in range(3)]
        turn_kept = [sem_of(f"turn_kept{c}") for c in range(3)]
        pv_done = sem_of("pv_done")
        q_ready = sem_of("q_ready")
        head_kept = sem_of("head_kept")
        att_turned = sem_of("att_turned")
        att_high = sem_of("att_high")
        att_low = sem_of("att_low")
        PARTS = [(0, 512), (512, 512), (1024, 256)]
        neg_max = stats[:, 16:18]
        prob_sum = stats[:, 18:20]
        prob_inv = stats[:, 20:22]

        def unit_head(i):
            return i // 2 + 4 * (i % 2)

        def att_tensor(pe):
            def scores(t, i, c):
                half, s = i % 2, i % 2
                at, n = PARTS[c]
                return nc.tensor.matmul(psum[:, 3 * s + c, 0:n], q_now[64 * half:64 * half + 64, i // 2, :],
                                        kT[64 * half:64 * half + 64, at:at + n], start=True, stop=True)

            def tile(t, last):
                for i in range(8):
                    s, n = i % 2, t * 4 + i // 2
                    pe.wait_ge(prob_done[s], n + 1)
                    for c, (at, width) in enumerate(PARTS):
                        if c:
                            pe.wait_ge(turn_kept[c - 1], t * 8 + (i + 1))
                        elif i == 0:
                            pe.wait_ge(att_low, t)
                        else:
                            pe.wait_ge(turn_kept[2], t * 8 + i)
                        for b in range(width // P):
                            mm = nc.tensor.transpose(psum[:, 6, b * P:(b + 1) * P], prob[:, s, at + b * P:at + (b + 1) * P], ident[:, :])
                        mm.then_inc(turn_done[c], 1)
                        if i < 6:
                            mm = scores(t, i + 2, c)
                        elif not last:
                            if i == 6 and c == 0:
                                pe.wait_ge(q_ready, t + 2)
                            mm = scores(t + 1, i - 6, c)
                    if not (last and i > 5):
                        mm.then_inc(score_done[s], 1)
                    for c in range(3):
                        pe.wait_ge(turn_kept[c], t * 8 + (i + 1))
                    pe.wait_ge(head_kept, t * 8 + i)
                    for b in range(KT):
                        mm = nc.tensor.matmul(psum[:, 7, 0:HD], probT[:, s, b * P:(b + 1) * P], vK[:, b, 64 * s:64 * s + 64], start=(b == 0), stop=(b == KT - 1))
                    mm.then_inc(pv_done, 1)
                pe.wait_ge(head_kept, t * 8 + 8)
                for b in range(4):
                    mm = nc.tensor.transpose(psum[:, 6, b * P:(b + 1) * P], att_out[:, 0, b * P:(b + 1) * P], ident[:, :])
                mm.then_inc(att_turned, 1)

            pe.wait_ge(q_ready, 1)
            for i in range(2):
                for c in range(3):
                    mm = scores(0, i, c)
                mm.then_inc(score_done[i], 1)
            latent_tiles(pe, tile)

        def latent_tiles(eng, tile, chain=None, per=0):
            with eng.Fori(0, SAMPLE_TILES - 1) as t:
                if chain:
                    chain.loop(t, per)
                tile(t, False)
            if chain:
                chain.end(SAMPLE_TILES - 1)
            tile(SAMPLE_TILES - 1, True)

        def att_gpsimd(pool):
            with pool.Fori(0, SAMPLE_TILES) as t:
                pool.wait_ge(score_done[1], t * 4)
                nc.gpsimd.tensor_copy(q_now[:, :, :], qT[:, :, tile_cols(t)]).then_inc(q_ready, 1)

        def att_scalar(act):
            def unit(t, i):
                s, n = i % 2, t * 4 + i // 2
                act.wait_ge(max_done[s], n + 1)
                nc.scalar.activation(prob[:, s, :], psum[:, 3 * s:3 * s + 3, :].rearrange("p b n -> p (b n)")[:, 0:KEYS], ACT.Exp,
                                     bias=neg_max[:, s:s + 1], accum_out=prob_sum[:, s:s + 1]).then_inc(prob_done[s], 1)

            def keep(t, i, c):
                at, width = PARTS[c]
                act.wait_ge(turn_done[c], t * 8 + (i + 1))
                nc.scalar.activation(probT[:, i % 2, at:at + width], psum[:, 6, 0:width], ACT.Copy).then_inc(turn_kept[c], 1)

            def tile(t, last):
                for i in range(8):
                    keep(t, i, 0)
                    if not (last and i == 7):
                        act.wait_ge(turn_kept[1], t * 8 + i)
                        unit(t if i < 7 else t + 1, (i + 1) % 8)
                    keep(t, i, 2)
                act.wait_ge(att_turned, t + 1)
                nc.scalar.activation(AT[:, 0, 0:4, tile_cols(t)], psum[:, 6, :].rearrange("p (b n) -> p b n", b=4), ACT.Copy).then_inc(att_high, 1)
            unit(0, 0)
            latent_tiles(act, tile)

        def att_vector(dve, chain):
            def biggest(t, i):
                s, n = i % 2, t * 4 + i // 2
                dve.wait_ge(score_done[s], n + 1)
                dve.wait_ge(prob_done[s], n)
                nc.vector.tensor_reduce(neg_max[:, s:s + 1], psum[:, 3 * s:3 * s + 3, :].rearrange("p b n -> p (b n)")[:, 0:KEYS], AX.X, ALU.max,
                                        negate=True).then_inc(max_done[s], 1)

            def head(t, i):
                s, n = i % 2, t * 4 + i // 2
                dve.wait_ge(prob_done[s], n + 1)
                dve.wait_ge(head_kept, t * 8 + i)
                chain.link(nc.vector.reciprocal(prob_inv[:, s:s + 1], prob_sum[:, s:s + 1]))
                dve.wait_ge(turn_done[1], t * 8 + (i + 1))
                nc.vector.tensor_copy(probT[:, s, 512:1024], psum[:, 6, :]).then_inc(turn_kept[1], 1)

            def out(t, i):
                s, h = i % 2, unit_head(i)
                dve.wait_ge(pv_done, t * 8 + (i + 1))
                if i == 0:
                    dve.wait_ge(att_turned, t)
                nc.vector.tensor_scalar(att_out[:, 0, h * HD:(h + 1) * HD], psum[:, 7, 0:HD], prob_inv[:, s:s + 1], None, ALU.mult).then_inc(head_kept, 1)

            def tile(t, last):
                for i in range(8):
                    if not (last and i == 7):
                        biggest(t if i < 7 else t + 1, (i + 1) % 8)
                    head(t, i)
                    out(t, i)
                dve.wait_ge(att_high, t + 1)
                nc.vector.tensor_tensor(AT[:, 1, 0:4, tile_cols(t)], psum[:, 6, :].rearrange("p (b n) -> p b n", b=4), ATf[:, 0, 0:4, tile_cols(t)],
                                        ALU.subtract).then_inc(att_low, 1)
            biggest(0, 0)
            latent_tiles(dve, tile, chain, 8)

        sem_of = Stage()
        ctx_scores = sem_of("ctx_scores")
        ctx_max = sem_of("ctx_max")
        ctx_prob = sem_of("ctx_prob")
        ctx_turned = sem_of("ctx_turned")
        ctx_kept = sem_of("ctx_kept")
        ctx_pv = sem_of("ctx_pv")
        ctx_out = sem_of("ctx_out")
        ctx_out_turned = sem_of("ctx_out_turned")
        ctx_high = sem_of("ctx_high")
        ctx_max_of = stats[:, 0:8]
        ctx_sum_of = stats[:, 8:16]
        cprob = prob[:].rearrange("p s n -> p (s n)")[:, 0:1024]
        cprobT = probT[:].rearrange("p s n -> p (s n)")[:, 0:1024]
        CTX0 = CTX * P

        def ctx_tensor(pe):
            for h in range(8):
                half = h // 4
                mm = nc.tensor.matmul(psum[:, half, (h % 4) * P:(h % 4 + 1) * P], qT[64 * half:64 * half + 64, h % 4, CTX0:CTX0 + P],
                                      kT[64 * half:64 * half + 64, KEYS:KEYS + P], start=True, stop=True)
            mm.then_inc(ctx_scores, 1)
            pe.wait_ge(ctx_prob, 1)
            for h in range(8):
                mm = nc.tensor.transpose(psum[:, 2 + h // 4, (h % 4) * P:(h % 4 + 1) * P], cprob[:, h * P:(h + 1) * P], ident[:, :])
            mm.then_inc(ctx_turned, 1)
            pe.wait_ge(ctx_kept, 1)
            for h in range(8):
                mm = nc.tensor.matmul(psum[:, 4, h * HD:(h + 1) * HD], cprobT[:, h * P:(h + 1) * P], vK[:, KT, 64 * (h // 4):64 * (h // 4) + 64], start=True, stop=True)
            mm.then_inc(ctx_pv, 1)
            pe.wait_ge(ctx_out, 1)
            for b in range(4):
                mm = nc.tensor.transpose(psum[:, 5, b * P:(b + 1) * P], att_out[:, 1, b * P:(b + 1) * P], ident[:, :])
            mm.then_inc(ctx_out_turned, 1)

        def ctx_scalar(act):
            act.wait_ge(ctx_max, 1)
            for i in range(8):
                ins = nc.scalar.activation(cprob[:, i * P:(i + 1) * P], psum[:, i // 4, (i % 4) * P:(i % 4 + 1) * P], ACT.Exp,
                                           bias=ctx_max_of[:, i:i + 1], accum_out=ctx_sum_of[:, i:i + 1])
            ins.then_inc(ctx_prob, 1)
            act.wait_ge(ctx_turned, 1)
            nc.scalar.activation(cprobT, psum[:, 2:4, :].rearrange("p b n -> p (b n)"), ACT.Copy).then_inc(ctx_kept, 1)
            act.wait_ge(ctx_out_turned, 1)
            nc.scalar.activation(AT[:, 0, 0:4, CTX0:CTX0 + P], psum[:, 5, :].rearrange("p (b n) -> p b n", b=4), ACT.Copy).then_inc(ctx_high, 1)

        def ctx_vector(dve, chain):
            dve.wait_ge(ctx_scores, 1)
            nc.vector.tensor_reduce(ctx_max_of, psum[:, 0:2, :].rearrange("p b (i n) -> p (b i) n", n=P), AX.X, ALU.max, negate=True).then_inc(ctx_max, 1)
            dve.wait_ge(ctx_prob, 1)
            chain.link(nc.vector.reciprocal(ctx_sum_of, ctx_sum_of))
            dve.wait_ge(ctx_pv, 1)
            for h in range(8):
                ins = nc.vector.tensor_scalar(att_out[:, 1, h * HD:(h + 1) * HD], psum[:, 4, h * HD:(h + 1) * HD], ctx_sum_of[:, h:h + 1], None, ALU.mult)
            ins.then_inc(ctx_out, 1)
            dve.wait_ge(ctx_high, 1)
            nc.vector.tensor_tensor(AT[:, 1, 0:4, CTX0:CTX0 + P], psum[:, 5, :].rearrange("p (b n) -> p b n", b=4), ATf[:, 0, 0:4, CTX0:CTX0 + P], ALU.subtract)

        R = 36
        SPAN = [slice(0, 4), slice(32, 36)]
        gate_at = Region(RAW0, END)
        neg_M = gate_at("neg_M", [R, T])
        tok = gate_at("tok", [P, 4, TILES, R])
        decay = gate_at("decay", [P, TILES, R])
        select = gate_at("select", [R, 8, P])
        mask = gate_at("mask", [P, 2, P])
        ml_shared = gate_at.at
        g_i = gate_at("g_i", [R, T])
        g_f = gate_at("g_f", [R, T])
        g_b = gate_at("g_b", [R, T])
        g_e = gate_at("g_e", [R, T])
        g_M = gate_at("g_M", [R, T])
        g_t = gate_at("g_t", [R, T])
        g_keep = gate_at("g_keep", [R, T])
        gateB = Region(WT0 + 32 * K, RAW0)
        g_raw = gateB("g_raw", [P, 2, TILES, R])
        g_bias = gateB("g_bias", [R, 2])
        g_m = gateB("g_m", [R, 12])
        g_last = gateB("g_last", [R, TILES])
        g_dec = gateB("g_dec", [R, TILES, R])
        sem_of = Stage()
        g_in = sem_of("g_in")
        g_clear = sem_of("g_clear")
        g_turned = sem_of("g_turned")
        g_kept = sem_of("g_kept")
        g_abs = sem_of("g_abs")
        g_soft = sem_of("g_soft")
        g_rows = sem_of("g_rows")
        g_back = sem_of("g_back")
        g_done = sem_of("g_done")
        m_out = sem_of("m_out")
        mask_step = sem_of("mask_step")

        def gates_sync(sp):
            sp.wait_ge(g_clear, 1)
            for w in range(2):
                for d in range(2):
                    sp.dma_start(g_raw[:, w, :, SPAN[d]], feat[0][:, :, 768 + 8 * w + 4 * d:768 + 8 * w + 4 * d + 4].rearrange("t p n -> p t n")).then_inc(g_in, 16)
            sp.dma_start(g_bias[:, :], A["gate_bias"]).then_inc(g_in, 16)
            sp.wait_ge(g_clear, 2)
            sp.dma_start(g_m[0:4, 0:1], A["m_start"][0]).then_inc(g_in, 16)
            sp.dma_start(g_m[32:36, 7:8], A["m_start"][1]).then_inc(g_in, 16)
            sp.wait_ge(g_rows, 1)
            for d in range(2):
                sp.dma_start(A["new_m"][d], g_m[SPAN[d], 10:11]).then_inc(m_out, 16)
            sp.wait_ge(m_out, 32)

        def gates_gpsimd(pool):
            nc.gpsimd.memset(g_raw[:, :, :, :], 0.0).then_inc(g_clear, 1)
            nc.gpsimd.memset(g_m[:, :], 0.0).then_inc(mask_step, 1)
            pool.wait_ge(mask_step, 1)
            nc.gpsimd.memset(g_m[:, 8:9], NEG).then_inc(g_clear, 1)
            nc.gpsimd.memset(mask[:, :, :], 0.0).then_inc(mask_step, 1)
            pool.wait_ge(mask_step, 2)
            nc.gpsimd.affine_select(out=mask[:, 0, :], in_=mask[:, 0, :], compare_op=ALU.is_ge, fill=NEG, base=0, pattern=[[1, P]], channel_multiplier=-1)
            nc.gpsimd.affine_select(out=mask[:, 1, :], in_=mask[:, 1, :], compare_op=ALU.is_ge, fill=NEG, base=0, pattern=[[-1, P]], channel_multiplier=1)
            nc.gpsimd.memset(g_keep[:, :], 1.0).then_inc(mask_step, 1)
            pool.wait_ge(mask_step, 3)
            nc.gpsimd.memset(g_keep[:].rearrange("p (t n) -> p t n", n=P)[:, :, 0:1], 0.0).then_inc(g_clear, 1)

        def gates_tensor(pe):
            pe.wait_ge(g_in, 16 * 7)
            for w in range(2):
                for t in range(TILES):
                    mm = nc.tensor.transpose(psum[0:R, 3 * w + t // 4, (t % 4) * P:(t % 4 + 1) * P], g_raw[:, w, t, :], ident[:, :])
            mm.then_inc(g_turned, 1)
            pe.wait_ge(g_rows, 1)
            for q, src in enumerate((g_e, g_t, g_f, g_i)):
                for t in range(TILES):
                    mm = nc.tensor.transpose(psum[:, q, t * R:(t + 1) * R], src[:, t * P:(t + 1) * P], ident[0:R, 0:R])
            nc.tensor.matmul(psum[:, 4, 0:TILES * R], ones[0:R, :], g_dec[:].rearrange("p t n -> p (t n)"), start=True, stop=True).then_inc(g_back, 1)

        def gates_scalar(act, chain):
            nc.scalar.preload_act_table_set("natural_log_exp_and_others")
            act.wait_ge(g_turned, 1)
            for w, dst in enumerate((g_i, g_f)):
                ins = nc.scalar.activation(dst[:, :], psum[0:R, 3 * w:3 * w + 3, :].rearrange("p b n -> p (b n)")[:, 0:T], ACT.Identity, bias=g_bias[:, w:w + 1])
            ins.then_inc(g_kept, 1)
            act.wait_ge(g_abs, 1)
            chain.link(nc.scalar.activation(g_t[:, :], g_t[:, :], ACT.Exp))
            nc.scalar.activation(g_t[:, :], g_t[:, :], ACT.Ln, bias=ones[0:R, 0:1]).then_inc(g_soft, 1)
            act.wait_ge(g_back, 1)
            for q in range(4):
                nc.scalar.activation(tok[:, q, :, :].rearrange("p t n -> p (t n)"), psum[:, q, 0:TILES * R], ACT.Exp if q else ACT.Copy)
            nc.scalar.activation(decay[:].rearrange("p t n -> p (t n)"), psum[:, 4, 0:TILES * R], ACT.Exp)

        def gates_vector(dve, chain):
            chain.link(nc.vector.memset(g_b[:, :], 0.0))
            chain.link(nc.vector.memset(g_M[:, :], 0.0))
            chain.link(nc.vector.memset(g_last[:, :], 0.0))
            for b in range(8):
                chain.mark(nc.vector.tensor_copy(select[:, b, :], ident[0:R, 32 * (b // 4) + b % 4:32 * (b // 4) + b % 4 + 1].to_broadcast([R, P])))
            dve.wait_ge(g_kept, 1)
            dve.wait_ge(g_clear, 3)
            nc.vector.scalar_tensor_tensor(g_t[:, :], g_f[:, :], -1.0, g_f[:, :], ALU.mult, ALU.min).then_inc(g_abs, 1)
            dve.wait_ge(g_soft, 1)
            chain.link(nc.vector.scalar_tensor_tensor(g_f[:, :], g_f[:, :], 0.0, g_t[:, :], ALU.min, ALU.subtract))
            chain.mark(nc.vector.tensor_tensor_scan(g_b[0:4, :], g_keep[0:4, :], g_f[0:4, :], 0.0, ALU.mult, ALU.add))
            chain.link(nc.vector.tensor_tensor_scan(g_b[32:36, ::-1], g_keep[32:36, :], g_f[32:36, ::-1], 0.0, ALU.mult, ALU.add))
            chain.link(nc.vector.tensor_tensor(g_e[:, :], g_i[:, :], g_b[:, :], ALU.subtract))
            for v in range(SAMPLE_TILES + 1):
                for d in range(2):
                    t = v if v == CTX or d == 0 else SAMPLE_TILES - 1 - v
                    rows_, lo, hi = SPAN[d], t * P, (t + 1) * P
                    last = hi - 1 if d == 0 else lo
                    nxt = 10 if t == CTX else 9 if v == SAMPLE_TILES - 1 else t + 1 - 2 * d
                    e, m = g_e[rows_, lo:hi], g_M[rows_, lo:hi]
                    if d:
                        e, m = g_e[rows_, lo:hi][:, ::-1], g_M[rows_, lo:hi][:, ::-1]
                    chain.link(nc.vector.tensor_tensor_scan(m, e, e, g_m[rows_, t:t + 1], ALU.max, ALU.max))
                    chain.mark(nc.vector.tensor_copy(g_last[rows_, t:t + 1], g_M[rows_, last:last + 1]))
                    chain.link(nc.vector.tensor_tensor(g_m[rows_, nxt:nxt + 1], g_b[rows_, last:last + 1], g_M[rows_, last:last + 1], ALU.add))
            tiles = lambda a: a[:].rearrange("p (t n) -> p t n", n=P)
            wide = lambda a: a.unsqueeze(2).to_broadcast([R, TILES, P])
            chain.mark(nc.vector.tensor_scalar(neg_M[:, :], g_M[:, :], -1.0, None, ALU.mult))
            chain.mark(nc.vector.tensor_tensor(tiles(g_t), wide(g_m[:, 0:TILES]), tiles(g_M), ALU.subtract))
            chain.mark(nc.vector.scalar_tensor_tensor(g_f[:, :], g_b[:, :], -1.0, g_M[:, :], ALU.mult, ALU.subtract))
            chain.link(nc.vector.tensor_tensor(tiles(g_i), tiles(g_e), wide(g_last[:, :]), ALU.subtract))
            chain.link(nc.vector.tensor_tensor(g_last[:, :], g_m[:, 0:TILES], g_last[:, :], ALU.subtract))
            nc.vector.tensor_tensor(g_dec[:, :, :], g_last[:, :].unsqueeze(2).to_broadcast([R, TILES, R]), ident[0:R, 0:R].unsqueeze(1).to_broadcast([R, TILES, R]),
                                    ALU.mult).then_inc(g_rows, 1)

        mlA = Region(WT0 + 32 * K, RAW0)
        h_sum = mlA("h_sum", [P, TILES, 512])
        C_n = mlA("C_n", [P, 8, MD + 1])
        mlB = Region(ml_shared, END)
        both = lambda n, shape, reg: [reg(f"{n}{d}", shape) for d in range(2)]
        ml_q = both("ml_q", [P, 4, P], mlB)
        ml_k = both("ml_k", [P, 4, P], mlB)
        ml_v = both("ml_v", [P, 4, MD + 1], mlB)
        ml_kT = both("ml_kT", [P, 4, P], mlB)
        ml_w = both("ml_w", [P, 4, P], mlB)
        ml_kw = both("ml_kw", [P, 4, P], mlB)
        ml_B = both("ml_B", [P, 4, MD + 1], mlB)
        ml_num = both("ml_num", [P, 4, MD + 1], mlB)
        ml_den = both("ml_den", [P, 4, 1], mlA)
        h_part = both("h_part", [P, 4, P], mlA)
        sem_of = Stage()
        two = lambda n: [sem_of(f"{n}{d}") for d in range(2)]
        ml_in, kt_sum, kt_kept, wb_sum, w_ready, ml_qk, ml_p = (two(n) for n in ("ml_in", "kt_sum", "kt_kept", "wb_sum", "w_ready", "ml_qk", "ml_p"))
        b_sum, b_kept, a_sum, num_ready, kw_ready, u_sum, c_ready, v_ones = (two(n) for n in ("b_sum", "b_kept", "a_sum", "num_ready", "kw_ready", "u_sum", "c_ready", "v_ones"))
        c_in = sem_of("c_in")
        c_out = sem_of("c_out")
        c_reset = sem_of("c_reset")
        h_clear = sem_of("h_clear")
        bank2 = lambda b: psum[:, b:b + 2, :].rearrange("p b (h n) -> p (b h) n", h=2)[:, :, 0:MD + 1]

        def steps(eng, body, chain=None, per=0):
            with eng.Fori(0, SAMPLE_TILES) as v:
                if chain:
                    chain.loop(v, per)
                body(v, (v, eng.compute_val(7 - v)))
            if chain:
                chain.end(SAMPLE_TILES)
            body(SAMPLE_TILES, (CTX, CTX))

        def ml_sync(sp):
            sp.dma_start(C_n[:, :, :], A["C_start"]).then_inc(c_in, 16)

            def body(v, tiles):
                for d in range(2):
                    sp.wait_ge(u_sum[d], v)
                    sp.dma_start(ml_k[d][:].rearrange("p h n -> p (h n)"), rows(feat[0], tiles[d])[:, 1296:1808]).then_inc(ml_in[d], 16)
                    sp.dma_start(ml_q[d][:, :, :], featT[0].rearrange("h p t -> p h t")[:, :, tile_cols(tiles[d])]).then_inc(ml_in[d], 16)
                    sp.dma_start(ml_v[d][:, :, 0:MD], rows(feat[0], tiles[d])[:, 1808:2320].rearrange("p (h n) -> p h n", h=4)).then_inc(ml_in[d], 16)
            steps(sp, body)
            for d in range(2):
                sp.wait_ge(c_ready[d], TILES)
            sp.dma_start(A["new_C"], C_n[:, :, :]).then_inc(c_out, 16)
            sp.wait_ge(c_out, 16)

        def ml_tensor(pe):
            pe.wait_ge(c_in, 16)
            for d in range(2):
                pe.wait_ge(v_ones[d], 1)

            def start(d, v, tile):
                pe.wait_ge(ml_in[d], v * 48 + 48)
                pe.wait_ge(ml_p[d], v)
                for h in range(4):
                    mm = nc.tensor.transpose(psum[:, d, h * P:(h + 1) * P], ml_k[d][:, h, :], ident[:, :])
                mm.then_inc(kt_sum[d], 1)
                pe.wait_ge(w_ready[d], v)
                for h in range(4):
                    nc.tensor.matmul(psum[:, 2 + d, h * P:(h + 1) * P], select[:, 4 * d + h, :], neg_M[:, tile_cols(tile)], start=True, stop=False)
                    mm = nc.tensor.matmul(psum[:, 2 + d, h * P:(h + 1) * P], ident[:, :], mask[:, d, :], start=False, stop=True)
                mm.then_inc(wb_sum[d], 1)

            def scores(d, v):
                pe.wait_ge(kt_kept[d], v + 1)
                for h in range(4):
                    mm = nc.tensor.matmul(psum[:, d, h * P:(h + 1) * P], ml_kT[d][:, h, :], ml_q[d][:, h, :], start=True, stop=True)
                mm.then_inc(ml_qk[d], 1)

            def from_state(d, v):
                pe.wait_ge(c_ready[d], v)
                pe.wait_ge(c_ready[1 - d], v + d)
                if isinstance(v, int):
                    pe.wait_ge(c_reset, 1)
                for h in range(4):
                    mm = nc.tensor.matmul(bank2(4)[:, h, :], ml_q[d][:, h, :], C_n[:, 4 * d + h, :], start=True, stop=True)
                mm.then_inc(b_sum[d], 1)

            def within(d, v):
                pe.wait_ge(ml_p[d], v + 1)
                pe.wait_ge(num_ready[1 - d], v + d)
                for h in range(4):
                    mm = nc.tensor.matmul(bank2(6)[:, h, :], ml_w[d][:, h, :], ml_v[d][:, h, :], start=True, stop=True)
                mm.then_inc(a_sum[d], 1)

            def into_state(d, v):
                pe.wait_ge(kw_ready[d], v + 1)
                pe.wait_ge(b_kept[d], v + 1)
                for h in range(4):
                    mm = nc.tensor.matmul(bank2(4)[:, h, :], ml_kw[d][:, h, :], ml_v[d][:, h, :], start=True, stop=True)
                mm.then_inc(u_sum[d], 1)

            def body(v, tiles):
                start(0, v, tiles[0])
                start(1, v, tiles[1])
                scores(0, v)
                from_state(0, v)
                scores(1, v)
                within(0, v)
                into_state(0, v)
                from_state(1, v)
                within(1, v)
                into_state(1, v)
            steps(pe, body)

        def ml_scalar(act):
            def body(v, tiles):
                for d in range(2):
                    act.wait_ge(kt_sum[d], v + 1)
                    nc.scalar.activation(ml_kT[d][:].rearrange("p h n -> p (h n)"), psum[:, d, :], ACT.Copy).then_inc(kt_kept[d], 1)
                    act.wait_ge(wb_sum[d], v + 1)
                    for h in range(4):
                        ins = nc.scalar.activation(ml_w[d][:, h, :], psum[:, 2 + d, h * P:(h + 1) * P], ACT.Exp, bias=tok[:, 0, ds(tiles[d], 1), 32 * d + h].rearrange("p a -> p a"))
                    ins.then_inc(w_ready[d], 1)
                for d in range(2):
                    act.wait_ge(b_sum[d], v + 1)
                    act.wait_ge(num_ready[d], v)
                    for h in range(4):
                        ins = nc.scalar.activation(ml_B[d][:, h, :], bank2(4)[:, h, :], ACT.Copy, scale=tok[:, 1, ds(tiles[d], 1), 32 * d + h])
                    ins.then_inc(b_kept[d], 1)
            steps(act, body)

        def ml_gpsimd(pool):
            for d in range(2):
                nc.gpsimd.memset(ml_v[d][:, :, MD:MD + 1], 1.0).then_inc(v_ones[d], 1)

            def body(v, tiles):
                for d in range(2):
                    pool.wait_ge(ml_in[d], v * 48 + 48)
                    pool.wait_ge(u_sum[d], v)
                    nc.gpsimd.tensor_tensor(ml_kw[d][:, :, :], ml_k[d][:, :, :], tok[:, 3, ds(tiles[d], 1), 32 * d:32 * d + 4].rearrange("p a h -> p (a h)").unsqueeze(2).to_broadcast([P, 4, P]),
                                            ALU.mult).then_inc(kw_ready[d], 1)
            steps(pool, body)

        def ml_vector(dve, chain):
            nc.vector.memset(h_sum[:, :, :], 0.0).then_inc(h_clear, 1)
            dve.wait_ge(h_clear, 1)
            dve.wait_ge(c_in, 16)
            def weigh(d, v):
                dve.wait_ge(ml_qk[d], v + 1)
                dve.wait_ge(w_ready[d], v + 1)
                w = ml_w[d][:].rearrange("p h n -> p (h n)")
                nc.vector.tensor_tensor(w, psum[:, d, :], w, ALU.mult).then_inc(ml_p[d], 1)

            def output(d, v, tile):
                dve.wait_ge(a_sum[d], v + 1)
                dve.wait_ge(b_kept[d], v + 1)
                num = ml_num[d]
                nc.vector.tensor_tensor(num[:, :, :], bank2(6), ml_B[d][:, :, :], ALU.add).then_inc(num_ready[d], 1)
                dve.wait_ge(num_ready[d], v + 1)
                chain.link(nc.vector.scalar_tensor_tensor(ml_den[d][:, :, :], num[:, :, MD:MD + 1], -1.0, num[:, :, MD:MD + 1], ALU.mult, ALU.max))
                chain.link(nc.vector.tensor_tensor(ml_den[d][:, :, :], ml_den[d][:, :, :], tok[:, 2, ds(tile, 1), 32 * d:32 * d + 4].rearrange("p a h -> p h a"), ALU.max))
                chain.link(nc.vector.reciprocal(ml_den[d][:, :, :], ml_den[d][:, :, :]))
                chain.link(nc.vector.tensor_tensor(h_part[d][:, :, :], num[:, :, 0:MD], ml_den[d][:, :, :].to_broadcast([P, 4, MD]), ALU.mult))
                hs = h_sum[:, ds(tile, 1), :].rearrange("p a n -> p (a n)")
                chain.link(nc.vector.tensor_tensor(hs, hs, h_part[d][:].rearrange("p h n -> p (h n)"), ALU.add))

            def update(d, v, tile):
                dve.wait_ge(u_sum[d], v + 1)
                for h in range(4):
                    C = C_n[:, 4 * d + h, :]
                    ins = nc.vector.scalar_tensor_tensor(C, C, decay[:, ds(tile, 1), 32 * d + h], bank2(4)[:, h, :], ALU.mult, ALU.add)
                ins.then_inc(c_ready[d], 1)

            def body(v, tiles):
                weigh(0, v)
                weigh(1, v)
                for d in range(2):
                    output(d, v, tiles[d])
                    update(d, v, tiles[d])

            with dve.Fori(0, SAMPLE_TILES) as v:
                chain.loop(v, 10)
                body(v, (v, dve.compute_val(7 - v)))
            chain.end(SAMPLE_TILES)
            for d in range(2):
                dve.wait_ge(c_ready[d], SAMPLE_TILES)
                dve.wait_ge(b_sum[d], SAMPLE_TILES)
            nc.vector.memset(C_n[:, :, :], 0.0).then_inc(c_reset, 1)
            dve.wait_ge(c_reset, 1)
            body(SAMPLE_TILES, (CTX, CTX))

        gate_cols = [slice(2320, 2832), slice(2048, 2560)]
        mlC = Region(ml_shared, END)
        mo_x = both("mo_x", [P, 512], mlC)
        mo_s = both("mo_s", [P, 512], mlC)
        mo_sq = both("mo_sq", [P, 4, P], mlC)
        mo_inv = both("mo_inv", [P, 4], mlC)
        mo_out = both("mo_out", [P, 512], mlC)
        mo_gain = mlC("mo_gain", [P, 512])
        sem_of = Stage()
        mo_gain_in = sem_of("mo_gain_in")
        mo_in, mo_ssq, mo_inv_ready, mo_exp, mo_ready, mo_turned, mo_high, mo_low = (
            two(n) for n in ("mo_in", "mo_ssq", "mo_inv_ready", "mo_exp", "mo_ready", "mo_turned", "mo_high", "mo_low"))

        def mo_sync(sp, l):
            sp.dma_start(mo_gain[:, :], A[("mlstm_gain", "gla_gain")[l]].to_broadcast([P, 512])).then_inc(mo_gain_in, 16)

            def body(tile, s, j):
                sp.wait_ge(mo_ready[s], j)
                sp.dma_start(mo_x[s][:, :], rows(feat[l], tile)[:, gate_cols[l]]).then_inc(mo_in[s], 16)
            pairs(sp, body)

        def mo_scalar(act, chain):
            nc.scalar.preload_act_table_set("natural_log_exp_and_others")
            def body(tile, s, j):
                act.wait_ge(mo_in[s], 16 * j + 16)
                act.wait_ge(mo_ready[s], j)
                nc.scalar.activation(mo_s[s][:, :], mo_x[s][:, :], ACT.Exp, scale=-1.0).then_inc(mo_exp[s], 1)
                act.wait_ge(mo_ssq[s], j + 1)
                chain.link(nc.scalar.activation(mo_inv[s][:, :], mo_inv[s][:, :], ACT.Ln, bias=eps[:, :], scale=1.0 / MD))
                nc.scalar.activation(mo_inv[s][:, :], mo_inv[s][:, :], ACT.Exp, scale=-0.5).then_inc(mo_inv_ready[s], 1)
                act.wait_ge(mo_turned[s], j + 1)
                nc.scalar.activation(AT[:, 0, 4:8, tile_cols(tile)], psum[:, s, :].rearrange("p (b n) -> p b n", b=4), ACT.Copy).then_inc(mo_high[s], 1)
            pairs(act, body, chain, 2)

        def mo_vector(dve, chain, l):
            dve.wait_ge(mo_gain_in, 16)

            def body(tile, s, j):
                hs = h_sum[:, ds(tile, 1), :].rearrange("p a n -> p (a n)")
                chain.link(nc.vector.tensor_tensor(mo_sq[s][:].rearrange("p h n -> p (h n)"), hs, hs, ALU.mult))
                nc.vector.tensor_reduce(mo_inv[s][:, :], mo_sq[s][:, :, :], AX.X, ALU.add).then_inc(mo_ssq[s], 1)
                dve.wait_ge(mo_exp[s], j + 1)
                chain.link(nc.vector.tensor_scalar(mo_s[s][:, :], mo_s[s][:, :], 1.0, None, ALU.add))
                chain.link(nc.vector.reciprocal(mo_s[s][:, :], mo_s[s][:, :]))
                chain.link(nc.vector.tensor_tensor(mo_s[s][:, :], mo_s[s][:, :], mo_gain[:, :], ALU.mult))
                if l:
                    chain.link(nc.vector.tensor_tensor(mo_s[s][:, :], mo_s[s][:, :], mo_x[s][:, :], ALU.mult))
                dve.wait_ge(mo_inv_ready[s], j + 1)
                dve.wait_ge(mo_turned[s], j)
                chain.link(nc.vector.tensor_tensor(mo_out[s][:].rearrange("p (h n) -> p h n", h=4), hs.rearrange("p (h n) -> p h n", h=4),
                                                   mo_inv[s][:, :].unsqueeze(2).to_broadcast([P, 4, P]), ALU.mult))
                nc.vector.tensor_tensor(mo_out[s][:, :], mo_out[s][:, :], mo_s[s][:, :], ALU.mult).then_inc(mo_ready[s], 1)
                dve.wait_ge(mo_high[s], j + 1)
                nc.vector.tensor_tensor(AT[:, 1, 4:8, tile_cols(tile)], psum[:, s, :].rearrange("p (b n) -> p b n", b=4), ATf[:, 0, 4:8, tile_cols(tile)],
                                        ALU.subtract).then_inc(mo_low[s], 1)
            pairs(dve, body, chain, (10, 12)[l])

        def mo_tensor(pe):
            def body(tile, s, j):
                pe.wait_ge(mo_ready[s], j + 1)
                pe.wait_ge(mo_low[s], j)
                for b in range(4):
                    mm = nc.tensor.transpose(psum[:, s, b * P:(b + 1) * P], mo_out[s][:, b * P:(b + 1) * P], ident[:, :])
                mm.then_inc(mo_turned[s], 1)
            pairs(pe, body)

        NS = SAMPLE_TILES * P
        CX = NS + 3
        LT = CX + P
        W3 = LT // 3
        SPARE = [slice(0, NS), slice(CX, LT)]
        TOK = [slice(0, NS), slice(NS, T)]
        lruB = Region(RAW0, END)
        lruA = Region(WT0 + 32 * K, RAW0)
        l_xp = lruB("l_xp", [P, LT + 3])
        l_xc = lruB("l_xc", [P, LT])
        l_g = lruB("l_g", [P, LT])
        l_t = lruB("l_t", [P, LT])
        l_r = both("l_r", [P, LT], lruB)
        l_i = both("l_i", [P, LT], lruB)
        l_a = both("l_a", [P, LT], lruB)
        l_w = both("l_w", [P, LT], lruA)
        l_h = both("l_h", [P, LT], lruA)
        l_mat = lruA("l_mat", [P, 4, P])
        l_bias = lruA("l_bias", [P, 4, 4])
        l_lam = lruA("l_lam", [P, 2, 4])
        l_rate = lruA("l_rate", [P, 2, 4])
        l_nrate = lruA("l_nrate", [P, 2, 4])
        l_conv = lruA("l_conv", [P, 4, 5])
        l_h0 = lruA("l_h0", [P, 2, 4])
        l_last = lruA("l_last", [P, 2, 4])
        sem_of = Stage()
        l_const_in = sem_of("l_const_in")
        l_clear = sem_of("l_clear")
        l_rated = sem_of("l_rated")
        l_abs = sem_of("l_abs")
        l_soft = sem_of("l_soft")
        l_in = sem_of("l_in")
        l_conv_ready = sem_of("l_conv_ready")
        l_sum, l_exp, l_sig, l_a_ready, l_w_ready, l_sqrt = (two(n) for n in ("l_sum", "l_exp", "l_sig", "l_a_ready", "l_w_ready", "l_sqrt"))
        l_sq = sem_of("l_sq")
        l_inner = sem_of("l_inner")
        l_tanh = sem_of("l_tanh")
        l_out_ready = sem_of("l_out_ready")
        l_high = sem_of("l_high")
        l_low = sem_of("l_low")
        l_states = sem_of("l_states")
        l_states_out = sem_of("l_states_out")
        GELU_A, GELU_B = 0.044715, float(np.sqrt(2.0 / np.pi))

        def lru_sync(sp):
            sp.dma_start(l_bias[:, :, :], A["lru_bias"]).then_inc(l_const_in, 16)
            sp.dma_start(l_lam[:, :, :], A["lru_lam"]).then_inc(l_const_in, 16)
            sp.dma_start(l_conv[:, :, :], A["lru_conv"]).then_inc(l_const_in, 16)
            sp.dma_start(l_h0[:, :, :], A["lru_h0"]).then_inc(l_const_in, 16)
            sp.wait_ge(l_clear, 2)
            with sp.Fori(0, 4) as c:
                sp.wait_ge(l_out_ready, c)
                for part in range(2):
                    tok_, pad = TOK[part], SPARE[part]
                    sp.dma_start(l_xp[:, pad.start + 2:pad.stop + 2], rows(featT[1], c)[:, tok_]).then_inc(l_in, 16)
                    sp.dma_start(l_g[:, pad], rows(featT[1], c + 4)[:, tok_]).then_inc(l_in, 16)
                sp.dma_start(l_mat[:, :, :], A["lru_mat"][ds(c, 1)].rearrange("a p g n -> (a p) g n")).then_inc(l_in, 16)
            sp.wait_ge(l_states, 4)
            sp.dma_start(A["new_h"], l_last[:, :, :]).then_inc(l_states_out, 16)
            sp.wait_ge(l_states_out, 16)

        def lru_tensor(pe):
            with pe.Fori(0, 4) as c:
                pe.wait_ge(l_conv_ready, c + 1)
                for d in range(2):
                    if d:
                        pe.wait_ge(l_exp[0], c + 1)
                    else:
                        pe.wait_ge(l_exp[1], c)
                    for g in range(2):
                        for b in range(3):
                            mm = nc.tensor.matmul(psum[:, 3 * g + b, 0:W3], l_mat[:, 2 * d + g, :], l_xc[:, b * W3:(b + 1) * W3], start=True, stop=True)
                    mm.then_inc(l_sum[d], 1)

        def lru_scalar(act, chain):
            act.wait_ge(l_abs, 1)
            chain.link(nc.scalar.activation(l_rate[:, :, :], l_rate[:, :, :], ACT.Exp))
            nc.scalar.activation(l_rate[:, :, :], l_rate[:, :, :], ACT.Ln, bias=ones[:, 0:1]).then_inc(l_soft, 1)
            act.wait_ge(l_rated, 1)
            with act.Fori(0, 4) as c:
                chain.loop(c, 2)
                for d in range(2):
                    act.wait_ge(l_sum[d], c + 1)
                    for g, dst in enumerate((l_r[d], l_i[d])):
                        ins = nc.scalar.activation(dst[:].rearrange("p (b n) -> p b n", b=3), psum[:, 3 * g:3 * g + 3, 0:W3], ACT.Exp, scale=-1.0,
                                                   bias=l_bias[:, ds(c, 1), 2 * d + g])
                    ins.then_inc(l_exp[d], 1)
                act.wait_ge(l_in, 80 * c + 80)
                act.wait_ge(l_low, c)
                nc.scalar.activation(l_t[:, :], l_g[:, :], ACT.Square).then_inc(l_sq, 1)
                for d in range(2):
                    act.wait_ge(l_sig[d], c + 1)
                    chain.link(nc.scalar.activation(l_a[d][:, :], l_r[d][:, :], ACT.Exp, scale=l_nrate[:, d, ds(c, 1)]))
                    nc.scalar.activation(l_w[d][:, :], l_r[d][:, :], ACT.Tanh, scale=l_rate[:, d, ds(c, 1)])
                    nc.scalar.activation(l_h[d][:, :], l_a[d][:, :], ACT.Square).then_inc(l_a_ready[d], 1)
                act.wait_ge(l_inner, c + 1)
                nc.scalar.activation(l_t[:, :], l_t[:, :], ACT.Tanh, scale=GELU_B).then_inc(l_tanh, 1)
                for d in range(2):
                    act.wait_ge(l_w_ready[d], c + 1)
                    nc.scalar.activation(l_w[d][:, :], l_w[d][:, :], ACT.Sqrt).then_inc(l_sqrt[d], 1)
                act.wait_ge(l_out_ready, c + 1)
                for part in range(2):
                    ins = nc.scalar.activation(AT[:, 0, ds(c, 1), TOK[part]].rearrange("p a n -> p (a n)"), l_h[0][:, SPARE[part]], ACT.Copy)
                ins.then_inc(l_high, 1)
            chain.end(4)

        def lru_gpsimd(pool):
            nc.gpsimd.memset(l_xp[:, :], 0.0).then_inc(l_clear, 1)
            nc.gpsimd.memset(l_g[:, :], 0.0).then_inc(l_clear, 1)
            with pool.Fori(0, 4) as c:
                pool.wait_ge(l_high, c + 1)
                for part in range(2):
                    ins = nc.gpsimd.tensor_tensor(AT[:, 1, ds(c, 1), TOK[part]].rearrange("p a n -> p (a n)"), l_h[0][:, SPARE[part]],
                                                  ATf[:, 0, ds(c, 1), TOK[part]].rearrange("p a n -> p (a n)"), ALU.subtract)
                ins.then_inc(l_low, 1)

        def lru_vector(dve, chain):
            dve.wait_ge(l_const_in, 64)
            chain.link(nc.vector.tensor_scalar(l_bias[:, :, :], l_bias[:, :, :], -1.0, None, ALU.mult))
            nc.vector.scalar_tensor_tensor(l_rate[:, :, :], l_lam[:, :, :], -1.0, l_lam[:, :, :], ALU.mult, ALU.min).then_inc(l_abs, 1)
            dve.wait_ge(l_soft, 1)
            chain.link(nc.vector.tensor_scalar(l_lam[:, :, :], l_lam[:, :, :], -1.0, 0.0, ALU.mult, ALU.max))
            chain.link(nc.vector.tensor_tensor(l_rate[:, :, :], l_rate[:, :, :], l_lam[:, :, :], ALU.add))
            chain.link(nc.vector.tensor_scalar(l_rate[:, :, :], l_rate[:, :, :], 8.0, None, ALU.mult))
            nc.vector.tensor_scalar(l_nrate[:, :, :], l_rate[:, :, :], -1.0, None, ALU.mult).then_inc(l_rated, 1)
            with dve.Fori(0, 4) as c:
                chain.loop(c, 18)
                dve.wait_ge(l_in, 80 * c + 80)
                tap = lambda j: l_conv[:, ds(c, 1), j]
                chain.link(nc.vector.tensor_scalar(l_xc[:, :], l_xp[:, 0:LT], tap(0), tap(4), ALU.mult, ALU.add))
                for j in (1, 2):
                    chain.link(nc.vector.scalar_tensor_tensor(l_xc[:, :], l_xp[:, j:j + LT], tap(j), l_xc[:, :], ALU.mult, ALU.add))
                nc.vector.scalar_tensor_tensor(l_xc[:, :], l_xp[:, 3:3 + LT], tap(3), l_xc[:, :], ALU.mult, ALU.add).then_inc(l_conv_ready, 1)
                for d in range(2):
                    dve.wait_ge(l_exp[d], c + 1)
                    for x in (l_r[d], l_i[d]):
                        chain.link(nc.vector.tensor_scalar(x[:, :], x[:, :], 1.0, None, ALU.add))
                    chain.mark(nc.vector.reciprocal(l_i[d][:, :], l_i[d][:, :]))
                    nc.vector.reciprocal(l_r[d][:, :], l_r[d][:, :]).then_inc(l_sig[d], 1)
                dve.wait_ge(l_sq, c + 1)
                chain.link(nc.vector.tensor_scalar(l_t[:, :], l_t[:, :], GELU_A, 1.0, ALU.mult, ALU.add))
                nc.vector.tensor_tensor(l_t[:, :], l_t[:, :], l_g[:, :], ALU.mult).then_inc(l_inner, 1)
                dve.wait_ge(l_conv_ready, c + 1)
                for d in range(2):
                    dve.wait_ge(l_a_ready[d], c + 1)
                    nc.vector.scalar_tensor_tensor(l_w[d][:, :], l_h[d][:, :], 1.0, l_w[d][:, :], ALU.add, ALU.mult).then_inc(l_w_ready[d], 1)
                    chain.mark(nc.vector.tensor_tensor(l_i[d][:, :], l_i[d][:, :], l_xc[:, :], ALU.mult))
                chain.sync()
                for d in range(2):
                    dve.wait_ge(l_sqrt[d], c + 1)
                    chain.link(nc.vector.tensor_tensor(l_i[d][:, :], l_i[d][:, :], l_w[d][:, :], ALU.mult))
                    rev = (lambda x: x[:, ::-1]) if d else (lambda x: x)
                    for part, start in ((0, l_h0[:, d, ds(c, 1)]), (1, 0.0)):
                        sl = SPARE[part]
                        ins = nc.vector.tensor_tensor_scan(rev(l_h[d][:, sl]), rev(l_a[d][:, sl]), rev(l_i[d][:, sl]), start, ALU.mult, ALU.add)
                        if part == 0 and d == 0:
                            continue
                    if d:
                        chain.link(ins)
                dve.wait_ge(l_tanh, c + 1)
                chain.link(nc.vector.scalar_tensor_tensor(l_t[:, :], l_t[:, :], 1.0, l_g[:, :], ALU.add, ALU.mult))
                nc.vector.tensor_copy(l_last[:, 0, ds(c, 1)], l_h[0][:, LT - 1:LT])
                nc.vector.tensor_copy(l_last[:, 1, ds(c, 1)], l_h[1][:, CX:CX + 1]).then_inc(l_states, 1)
                dve.wait_ge(l_states, c + 1)
                chain.link(nc.vector.tensor_tensor(l_h[0][:, SPARE[0]], l_h[0][:, SPARE[0]], l_h[1][:, SPARE[0]], ALU.add))
                chain.link(nc.vector.tensor_tensor(l_h[0][:, SPARE[1]], l_h[0][:, SPARE[1]], l_h[1][:, SPARE[1]], ALU.add))
                for part in range(2):
                    sl = SPARE[part]
                    ins = nc.vector.scalar_tensor_tensor(l_h[0][:, sl], l_h[0][:, sl], 0.5, l_t[:, sl], ALU.mult, ALU.mult)
                ins.then_inc(l_out_ready, 1)
            chain.end(4)

        LEVELS = [P >> n for n in range(7)]
        NL = len(LEVELS)
        TAU = 16.0
        GT = P + 1
        glB = Region(RAW0, END)
        gate_sum = glB("gate_sum", [P, 4, TILES, GT])
        gl_shared = glB.at
        gl_log = glB("gl_log", [P, 4, TILES, GT])
        gl_low_rank = glB("gl_low_rank", [32, T])
        gl_w = glB("gl_w", [32, 4, P])
        gl_b = glB("gl_b", [P, 4])
        gl_keep = Region(WT0 + 52 * K, RAW0)("gl_keep", [P, TILES, GT])
        sem_of = Stage()
        gl_in = sem_of("gl_in")
        gl_clear = sem_of("gl_clear")
        gl_keep_ready = sem_of("gl_keep_ready")
        gl_z = [sem_of(f"gl_z{n}") for n in range(2)]
        gl_z_kept = [sem_of(f"gl_z_kept{n}") for n in range(2)]
        gl_abs = sem_of("gl_abs")
        gl_soft = sem_of("gl_soft")

        def decay_sync(sp):
            sp.dma_start(gl_low_rank[:, :], featT[1][12, 0:32, :]).then_inc(gl_in, 16)
            sp.dma_start(gl_w[:, :, :], A["gla_w"]).then_inc(gl_in, 16)
            sp.dma_start(gl_b[:, :], A["gla_b"]).then_inc(gl_in, 16)

        def decay_gpsimd(pool):
            nc.gpsimd.memset(gate_sum[:, :, :, 0:1], 0.0).then_inc(gl_clear, 1)
            nc.gpsimd.memset(gl_keep[:, :, :], 1.0).then_inc(gl_keep_ready, 1)
            pool.wait_ge(gl_keep_ready, 1)
            nc.gpsimd.memset(gl_keep[:, :, 0:1], 0.0).then_inc(gl_keep_ready, 1)

        def decay_tensor(pe):
            pe.wait_ge(gl_in, 48)
            for n in range(4):
                pe.wait_ge(gl_z_kept[n % 2], n // 2) if n > 1 else None
                for b in range(3):
                    mm = nc.tensor.matmul(psum[:, 3 * (n % 2) + b, 0:TB], gl_w[:, n, :], gl_low_rank[:, b * TB:(b + 1) * TB], start=True, stop=True)
                mm.then_inc(gl_z[n % 2], 1)

        def decay_scalar(act, chain):
            for n in range(4):
                act.wait_ge(gl_z[n % 2], n // 2 + 1)
                nc.scalar.activation(gate_sum[:, n, :, :].rearrange("p (b t) n -> p b t n", b=3)[:, :, :, 1:GT],
                                     psum[:, 3 * (n % 2):3 * (n % 2) + 3, 0:TB].rearrange("p b (t n) -> p b t n", t=3), ACT.Identity,
                                     bias=gl_b[:, n:n + 1]).then_inc(gl_z_kept[n % 2], 1)
            act.wait_ge(gl_abs, 1)
            flat = gl_log[:].rearrange("p c t n -> p (c t n)")
            chain.link(nc.scalar.activation(flat, flat, ACT.Exp))
            nc.scalar.activation(flat, flat, ACT.Ln, bias=ones[:, 0:1]).then_inc(gl_soft, 1)

        def decay_vector(dve, chain):
            dve.wait_ge(gl_clear, 1)
            for n in range(2):
                dve.wait_ge(gl_z_kept[n], 2)
            z, la = gate_sum[:].rearrange("p c t n -> p (c t n)"), gl_log[:].rearrange("p c t n -> p (c t n)")
            nc.vector.scalar_tensor_tensor(la, z, -1.0, z, ALU.mult, ALU.min).then_inc(gl_abs, 1)
            dve.wait_ge(gl_soft, 1)
            chain.link(nc.vector.scalar_tensor_tensor(la, z, 0.0, la, ALU.min, ALU.subtract))
            chain.link(nc.vector.tensor_scalar(la, la, 1.0 / TAU, None, ALU.mult))
            chain.link(nc.vector.memset(gl_log[:, :, :, 0:1], 0.0))
            dve.wait_ge(gl_keep_ready, 2)
            for n in range(4):
                flat = lambda a: a.rearrange("p t n -> p (t n)")
                nc.vector.tensor_tensor_scan(flat(gate_sum[:, n, :, :]), flat(gl_keep[:, :, :]), flat(gl_log[:, n, :, :]), 0.0, ALU.mult, ALU.add)

        glS = Region(gl_shared, END)
        level_mask = glS("level_mask", [P, NL, P], mybir.dt.int32)
        gl_kqk = both("gl_kqk", [P, 6, P], glS)
        gl_v = both("gl_v", [P, 512], glS)
        gl_V = both("gl_V", [P, 4, P], glS)
        gl_I = both("gl_I", [P, 4, P], glS)
        gl_E = both("gl_E", [P, 4, P], glS)
        gl_F = both("gl_F", [P, 4, P], glS)
        wsum = both("wsum", [P, 4, P], glS)
        sem_of = Stage()
        two = lambda n: [sem_of(f"{n}{d}") for d in range(2)]
        wi_mask_in = sem_of("wi_mask_in")
        wi_in, wi_V, wi_D, wi_E, wi_F, wi_mm, wi_put, wi_o, wi_o_kept = (
            two(n) for n in ("wi_in", "wi_V", "wi_D", "wi_E", "wi_F", "wi_mm", "wi_put", "wi_o", "wi_o_kept"))
        halves = lambda a, B: a.rearrange("p c (b n) -> p c b n", n=B)
        per_step = lambda n, step: n * 4 + step // 2
        per_level = lambda n, step: n * (3, 4)[step % 2] + (step - 1) // 2

        def within_sync(sp):
            sp.dma_start(level_mask[:, :, :], A["level_mask"]).then_inc(wi_mask_in, 16)

            def body(tile, s, j):
                sp.wait_ge(wi_o[s], j)
                for n, at in enumerate((10, 8, 10)):
                    sp.dma_start(gl_kqk[s][:, 2 * n:2 * n + 2, :], featT[1][at:at + 2].rearrange("a p t -> p a t")[:, :, tile_cols(tile)]).then_inc(wi_in[s], 16)
                sp.dma_start(gl_v[s][:, :], rows(feat[1], tile)[:, 1536:2048]).then_inc(wi_in[s], 16)
            pairs(sp, body)

        def within_gpsimd(pool):
            def body(tile, s, j):
                pool.wait_ge(wi_D[1], j * 8 + 4 * s)
                for d in range(2):
                    nc.gpsimd.tensor_copy(gl_V[s][:, 2 * d:2 * d + 2, :], gate_sum[:, 2 * d:2 * d + 2, ds(tile, 1), 1 - d:GT - d].rearrange("p c a n -> p (c a) n"))
                nc.gpsimd.tensor_copy(gl_I[s][:, :, :], gate_sum[:, :, ds(tile, 1), 1:GT].rearrange("p c a n -> p (c a) n")).then_inc(wi_V[s], 1)
                pool.wait_ge(wi_V[s], j + 1)
                for step in range(1, NL + 1):
                    B, p = LEVELS[step - 1], step % 2
                    H = B // 2
                    E, V = halves(gl_E[p][:, :, :], B), halves(gl_V[s][:, :, :], B)
                    ref = halves(gl_I[s][:, :, :], B)[:, :, :, H - 1:H].to_broadcast([P, 4, P // B, H])
                    pool.wait_ge(wi_F[p], per_level(j * 2 + s, step))
                    nc.gpsimd.tensor_tensor(E[:, :, :, 0:H], ref, V[:, :, :, 0:H], ALU.subtract)
                    nc.gpsimd.tensor_tensor(E[:, :, :, H:B], V[:, :, :, H:B], ref, ALU.subtract).then_inc(wi_D[p], 1)
            pairs(pool, body)

        def within_scalar(act):
            def body(tile, s, j):
                for step in range(1, NL + 1):
                    p = step % 2
                    act.wait_ge(wi_D[p], per_level(j * 2 + s, step) + 1)
                    nc.scalar.activation(gl_E[p][:, :, :], gl_E[p][:, :, :], ACT.Exp).then_inc(wi_E[p], 1)
                act.wait_ge(wi_o[s], j + 1)
                nc.scalar.activation(h_sum[:, ds(tile, 1), :].rearrange("p a n -> p (a n)"), psum[:, 4 + s, :], ACT.Copy, scale=GK ** -0.5).then_inc(wi_o_kept[s], 1)
            pairs(act, body)

        def within_vector(dve):
            def factors(tile, s, j, step):
                if step:
                    B, p = LEVELS[step - 1], step % 2
                    H = B // 2
                    F, E, G = halves(gl_F[p][:, :, :], B), halves(gl_E[p][:, :, :], B), halves(gl_kqk[s][:, :, :], B)
                    dve.wait_ge(wi_E[p], per_level(j * 2 + s, step) + 1)
                    dve.wait_ge(wi_mm[p], per_step(j * 2 + s, step))
                    nc.vector.tensor_tensor(F[:, :, :, 0:H], E[:, :, :, 0:H], G[:, 0:4, :, 0:H], ALU.mult)
                    nc.vector.tensor_tensor(F[:, :, :, H:B], E[:, :, :, H:B], G[:, 2:6, :, H:B], ALU.mult).then_inc(wi_F[p], 1)

            def put(tile, s, j, step):
                p = step % 2
                out = wsum[s][:, :, :]
                prod = psum[:, 2 * p:2 * p + 2, :].rearrange("p a (c n) -> p (a c) n", c=2)[:, :, 0:P]
                dve.wait_ge(wi_mm[p], per_step(j * 2 + s, step) + 1)
                wide = lambda m: m.unsqueeze(1).to_broadcast([P, 4, P])
                if step == 0:
                    nc.vector.scalar_tensor_tensor(out, prod, 2.0, wide(ident[:, :]), ALU.mult, ALU.mult).then_inc(wi_put[p], 1)
                else:
                    nc.vector.copy_predicated(out, wide(level_mask[:, step - 1, :]), prod).then_inc(wi_put[p], 1)

            def body(tile, s, j):
                dve.wait_ge(wi_in[s], 64 * j + 64)
                dve.wait_ge(wi_o[s], j)
                factors(tile, s, j, 1)
                for step in range(NL + 1):
                    if step + 2 <= NL:
                        factors(tile, s, j, step + 2)
                    dve.wait_ge(wi_mask_in, 16)
                    if step:
                        dve.wait_ge(wi_put[(step - 1) % 2], per_step(j * 2 + s, step - 1) + 1)
                    put(tile, s, j, step)
            pairs(dve, body)

        def within_tensor(pe):
            def body(tile, s, j):
                pe.wait_ge(wi_in[s], 64 * j + 64)
                for step in range(NL + 1):
                    p = step % 2
                    pe.wait_ge(wi_put[p], per_step(j * 2 + s, step))
                    if step:
                        pe.wait_ge(wi_F[p], per_level(j * 2 + s, step) + 1)
                    for par in range(2):
                        r = slice(64 * par, 64 * par + 64)
                        for ct in range(2):
                            out = psum[:, 2 * p + par, 2 * ct * P:(2 * ct + 1) * P]
                            if step == 0:
                                mm = nc.tensor.matmul(out, gl_kqk[s][r, ct, :], gl_kqk[s][r, 2 + ct, :], start=True, stop=True)
                                continue
                            B = LEVELS[step - 1]
                            H = B // 2
                            blocks = lambda a: a.rearrange("p (b n) -> p b n", n=B)
                            for d, cols in ((0, slice(H, B)), (1, slice(0, H))):
                                F = gl_F[p][r, 2 * d + ct, :]
                                mm = nc.tensor.matmul(blocks(out)[:, :, cols], F, blocks(F)[:, :, cols], start=True, stop=True)
                    mm.then_inc(wi_mm[p], 1)
                for q in range(2):
                    pe.wait_ge(wi_put[q], per_step(j * 2 + s, 6 + q) + 1)
                pe.wait_ge(wi_o_kept[s], j)
                for h in range(4):
                    mm = nc.tensor.matmul(psum[:, 4 + s, h * P:(h + 1) * P], wsum[s][:, 2 * (h % 2) + h // 2, :], gl_v[s][:, h * P:(h + 1) * P], start=True, stop=True)
                mm.then_inc(wi_o[s], 1)
            pairs(pe, body)

        glT = Region(gl_shared, END)
        gl_S = glT("gl_S", [P, 4, 2 * P])
        gt_kq = both("gt_kq", [P, 4, P], glT)
        gt_v = both("gt_v", [P, 512], glT)
        gt_E = both("gt_E", [P, 4, P], glT)
        gt_W = both("gt_W", [P, 4, P], glT)
        gt_kT = both("gt_kT", [P, 2, P], glT)
        gt_decay = both("gt_decay", [P, 2], glT)
        sem_of = Stage()
        two = lambda n: [sem_of(f"{n}{d}") for d in range(2)]
        gt_in, gt_exp, gt_weighed, gt_turned, gt_kT_kept, gt_o, gt_o_kept, gt_u, gt_S_new = (
            two(n) for n in ("gt_in", "gt_exp", "gt_weighed", "gt_turned", "gt_kT_kept", "gt_o", "gt_o_kept", "gt_u", "gt_S_new"))
        S_clear = sem_of("S_clear")
        S_in = sem_of("S_in")
        S_out = sem_of("S_out")
        S_reset = sem_of("S_reset")

        def state_sync(sp):
            sp.wait_ge(S_clear, 1)
            for par in range(2):
                sp.dma_start(gl_S[64 * par:64 * par + 64, :, par * P:(par + 1) * P], A["gla_S"][par]).then_inc(S_in, 16)

            def body(v, tiles):
                for d in range(2):
                    sp.wait_ge(gt_u[d], v)
                    sp.wait_ge(gt_weighed[d], v)
                    for n, at in enumerate((10, 8)):
                        sp.dma_start(gt_kq[d][:, 2 * n:2 * n + 2, :], featT[1][at:at + 2].rearrange("a p t -> p a t")[:, :, tile_cols(tiles[d])]).then_inc(gt_in[d], 16)
                    sp.dma_start(gt_v[d][:, :], rows(feat[1], tiles[d])[:, 1536:2048]).then_inc(gt_in[d], 16)
            steps(sp, body)
            for d in range(2):
                sp.wait_ge(gt_S_new[d], TILES)
            for par in range(2):
                sp.dma_start(A["new_S"][par], gl_S[64 * par:64 * par + 64, :, par * P:(par + 1) * P]).then_inc(S_out, 16)
            sp.wait_ge(S_out, 32)

        def state_scalar(act):
            def body(v, tiles):
                for d in range(2):
                    act.wait_ge(gt_weighed[d], v)
                    act.wait_ge(gt_S_new[d], v)
                    V = gate_sum[:, 2 * d:2 * d + 2, ds(tiles[d], 1), 1 - d:GT - d].rearrange("p c a n -> p (c a) n")
                    end = gate_sum[:, 2 * d:2 * d + 2, ds(tiles[d], 1), P:GT].rearrange("p c a n -> p (c a n)")
                    nc.scalar.activation(gt_E[d][:, 2 - 2 * d:4 - 2 * d, :], V, ACT.Exp)
                    nc.scalar.activation(gt_decay[d][:, :], end, ACT.Exp)
                    for ct in range(2):
                        ins = nc.scalar.activation(gt_E[d][:, 2 * d + ct, :], V[:, ct, :], ACT.Exp, scale=-1.0, bias=end[:, ct:ct + 1])
                    ins.then_inc(gt_exp[d], 1)
                for d in range(2):
                    act.wait_ge(gt_turned[d], v + 1)
                    act.wait_ge(gt_u[d], v)
                    nc.scalar.activation(gt_kT[d][:].rearrange("p c n -> p (c n)"), psum[:, d, 0:2 * P], ACT.Copy).then_inc(gt_kT_kept[d], 1)
            steps(act, body)

        def state_gpsimd(pool):
            nc.gpsimd.memset(gl_S[:, :, :], 0.0).then_inc(S_clear, 1)

            def body(v, tiles):
                for d in range(2):
                    pool.wait_ge(gt_exp[d], v + 1)
                    pool.wait_ge(gt_in[d], v * 48 + 48)
                    pool.wait_ge(gt_turned[d], v)
                    pool.wait_ge(gt_o[d], v)
                    nc.gpsimd.tensor_tensor(gt_W[d][:, :, :], gt_E[d][:, :, :], gt_kq[d][:, :, :], ALU.mult).then_inc(gt_weighed[d], 1)
            steps(pool, body)

        def state_tensor(pe):
            pe.wait_ge(S_in, 32)

            def body(v, tiles):
                for d in range(2):
                    pe.wait_ge(gt_weighed[d], v + 1)
                    pe.wait_ge(gt_kT_kept[d], v)
                    for ct in range(2):
                        mm = nc.tensor.transpose(psum[:, d, ct * P:(ct + 1) * P], gt_W[d][:, ct, :], ident[:, :])
                    mm.then_inc(gt_turned[d], 1)
                for d in range(2):
                    pe.wait_ge(gt_S_new[d], v)
                    pe.wait_ge(gt_o_kept[d], v)
                    if isinstance(v, int):
                        pe.wait_ge(S_reset, 1)
                    for ct in range(2):
                        mm = nc.tensor.matmul(psum[:, 2 + d, 2 * ct * P:2 * (ct + 1) * P], gt_W[d][:, 2 + ct, :], gl_S[:, 2 * d + ct, :], start=True, stop=True)
                    mm.then_inc(gt_o[d], 1)
                    pe.wait_ge(gt_kT_kept[d], v + 1)
                    pe.wait_ge(gt_in[d], v * 48 + 48)
                    for ct in range(2):
                        mm = nc.tensor.matmul(psum[:, 4 + d, 2 * ct * P:2 * (ct + 1) * P], gt_kT[d][:, ct, :], gt_v[d][:, 2 * ct * P:2 * (ct + 1) * P], start=True, stop=True)
                    mm.then_inc(gt_u[d], 1)
            steps(pe, body)

        def state_vector(dve):
            dve.wait_ge(S_in, 32)

            def body(v, tiles):
                for d in range(2):
                    dve.wait_ge(gt_o[d], v + 1)
                    dve.wait_ge(gt_o_kept[1 - d], v + d)
                    hs = h_sum[:, ds(tiles[d], 1), :].rearrange("p a n -> p (a n)")
                    nc.vector.scalar_tensor_tensor(hs, psum[:, 2 + d, :], GK ** -0.5, hs, ALU.mult, ALU.add).then_inc(gt_o_kept[d], 1)
                    dve.wait_ge(gt_u[d], v + 1)
                    dve.wait_ge(gt_exp[d], v + 1)
                    for ct in range(2):
                        for par in range(2):
                            r, c = slice(64 * par, 64 * par + 64), slice(par * P, (par + 1) * P)
                            S = gl_S[r, 2 * d + ct, c]
                            ins = nc.vector.scalar_tensor_tensor(S, S, gt_decay[d][r, ct:ct + 1], psum[r, 4 + d, (2 * ct + par) * P:(2 * ct + par + 1) * P], ALU.mult, ALU.add)
                    ins.then_inc(gt_S_new[d], 1)

            with dve.Fori(0, SAMPLE_TILES) as v:
                body(v, (v, dve.compute_val(7 - v)))
            for d in range(2):
                dve.wait_ge(gt_S_new[d], SAMPLE_TILES)
                dve.wait_ge(gt_o[d], SAMPLE_TILES)
            nc.vector.memset(gl_S[:, :, :], 0.0).then_inc(S_reset, 1)
            dve.wait_ge(S_reset, 1)
            body(SAMPLE_TILES, (CTX, CTX))


        def mixer_sync(sp, l):
            if l == 0:
                qk_sync(sp)
                next_stage(sp, "query and key norms")
                next_stage(sp, "latent attention")
                next_stage(sp, "context attention")
                gates_sync(sp)
                next_stage(sp, "mLSTM gates")
                ml_sync(sp)
                next_stage(sp, "mLSTM chunks")
                mo_sync(sp, l)
                next_stage(sp, "mLSTM output")
            else:
                lru_sync(sp)
                next_stage(sp, "RG-LRU")
                decay_sync(sp)
                next_stage(sp, "GLA decays")
                within_sync(sp)
                next_stage(sp, "GLA within chunks")
                state_sync(sp)
                next_stage(sp, "GLA states")
                mo_sync(sp, l)
                next_stage(sp, "GLA output")

        def mixer_gpsimd(pool, l):
            if l == 0:
                next_stage(pool, "query and key norms", clear=True)
                att_gpsimd(pool)
                next_stage(pool, "latent attention", clear=True)
                next_stage(pool, "context attention", clear=True)
                gates_gpsimd(pool)
                next_stage(pool, "mLSTM gates", clear=True)
                ml_gpsimd(pool)
                next_stage(pool, "mLSTM chunks", clear=True)
                next_stage(pool, "mLSTM output", clear=True)
            else:
                lru_gpsimd(pool)
                next_stage(pool, "RG-LRU", clear=True)
                decay_gpsimd(pool)
                next_stage(pool, "GLA decays", clear=True)
                within_gpsimd(pool)
                next_stage(pool, "GLA within chunks", clear=True)
                state_gpsimd(pool)
                next_stage(pool, "GLA states", clear=True)
                next_stage(pool, "GLA output", clear=True)

        def mixer_scalar(act, chain, l):
            if l == 0:
                qk_scalar(act, chain)
                next_stage(act, "query and key norms")
                att_scalar(act)
                next_stage(act, "latent attention")
                ctx_scalar(act)
                next_stage(act, "context attention")
                gates_scalar(act, chain)
                next_stage(act, "mLSTM gates")
                ml_scalar(act)
                next_stage(act, "mLSTM chunks")
                mo_scalar(act, chain)
                next_stage(act, "mLSTM output")
            else:
                lru_scalar(act, chain)
                next_stage(act, "RG-LRU")
                decay_scalar(act, chain)
                next_stage(act, "GLA decays")
                within_scalar(act)
                next_stage(act, "GLA within chunks")
                state_scalar(act)
                next_stage(act, "GLA states")
                mo_scalar(act, chain)
                next_stage(act, "GLA output")

        def mixer_tensor(pe, l):
            if l == 0:
                qk_tensor(pe)
                next_stage(pe, "query and key norms")
                att_tensor(pe)
                next_stage(pe, "latent attention")
                ctx_tensor(pe)
                next_stage(pe, "context attention")
                gates_tensor(pe)
                next_stage(pe, "mLSTM gates")
                ml_tensor(pe)
                next_stage(pe, "mLSTM chunks")
                mo_tensor(pe)
                next_stage(pe, "mLSTM output")
            else:
                lru_tensor(pe)
                next_stage(pe, "RG-LRU")
                decay_tensor(pe)
                next_stage(pe, "GLA decays")
                within_tensor(pe)
                next_stage(pe, "GLA within chunks")
                state_tensor(pe)
                next_stage(pe, "GLA states")
                mo_tensor(pe)
                next_stage(pe, "GLA output")

        def mixer_vector(dve, chain, l):
            if l == 0:
                qk_vector(dve, chain)
                next_stage(dve, "query and key norms")
                att_vector(dve, chain)
                next_stage(dve, "latent attention")
                ctx_vector(dve, chain)
                next_stage(dve, "context attention")
                gates_vector(dve, chain)
                next_stage(dve, "mLSTM gates")
                ml_vector(dve, chain)
                next_stage(dve, "mLSTM chunks")
                mo_vector(dve, chain, l)
                next_stage(dve, "mLSTM output")
            else:
                lru_vector(dve, chain)
                next_stage(dve, "RG-LRU")
                decay_vector(dve, chain)
                next_stage(dve, "GLA decays")
                within_vector(dve)
                next_stage(dve, "GLA within chunks")
                state_vector(dve)
                next_stage(dve, "GLA states")
                mo_vector(dve, chain, l)
                next_stage(dve, "GLA output")

        def ada_groups(eng, part, l=0):
            with eng.Fori(0, 6) as j:
                for s in range(2):
                    part(eng, l, s, j)

        block = st.enter_context(nc.Block())

        @block.sync
        def _(sp):
            const_sync(sp)
            barrier(sp, "constants")
            ada_sync(sp)
            barrier(sp, "adaln 0")
            for l in range(LAYERS):
                if l == 0:
                    pass_sync(sp, 0)
                    barrier(sp, "first norm")
                proj_sync(sp, l)
                barrier(sp, f"in-projection {l}")
                mixer_sync(sp, l)
                barrier(sp, f"mixer {l}")
                barrier(sp, f"mixer gate {l}")
                pass_sync(sp, 2 * l + 1)
                barrier(sp, f"mixer output {l}")
                mlp_sync(sp, l)
                barrier(sp, f"mlp {l}")
                barrier(sp, f"mlp gate {l}")
                pass_sync(sp, 2 * l + 2)
                barrier(sp, f"mlp output {l}")

        @block.gpsimd
        def _(pool):
            const_gpsimd(pool)
            barrier(pool, "constants")
            pool.wait_ge(silu_ready, 1)
            ada_groups(pool, ada_gpsimd)
            barrier(pool, "adaln 0")
            for l in range(LAYERS):
                if l == 0:
                    pass_gpsimd(pool, 0)
                    barrier(pool, "first norm")
                proj_gpsimd(pool, l)
                barrier(pool, f"in-projection {l}")
                mixer_gpsimd(pool, l)
                barrier(pool, f"mixer {l}")
                barrier(pool, f"mixer gate {l}")
                pass_gpsimd(pool, 2 * l + 1)
                barrier(pool, f"mixer output {l}")
                mlp_gpsimd(pool, l)
                barrier(pool, f"mlp {l}")
                barrier(pool, f"mlp gate {l}")
                pass_gpsimd(pool, 2 * l + 2)
                barrier(pool, f"mlp output {l}")

        @block.scalar
        def _(act):
            chain = Chain(act, achain_sem)
            silu_scalar(act)
            barrier(act, "constants")
            act.wait_ge(silu_ready, 1)
            ada_groups(act, ada_scalar)
            barrier(act, "adaln 0")
            for l in range(LAYERS):
                if l == 0:
                    pass_scalar(act, chain, 0)
                    barrier(act, "first norm")
                proj_scalar(act, l)
                barrier(act, f"in-projection {l}")
                mixer_scalar(act, chain, l)
                barrier(act, f"mixer {l}")
                gate_scalar(act, l, 0)
                barrier(act, f"mixer gate {l}")
                pass_scalar(act, chain, 2 * l + 1)
                barrier(act, f"mixer output {l}")
                mlp_scalar(act, l)
                barrier(act, f"mlp {l}")
                gate_scalar(act, l, 1)
                barrier(act, f"mlp gate {l}")
                pass_scalar(act, chain, 2 * l + 2)
                barrier(act, f"mlp output {l}")

        @block.tensor
        def _(pe):
            barrier(pe, "constants")
            ada_tensor(pe)
            barrier(pe, "adaln 0")
            for l in range(LAYERS):
                if l == 0:
                    pass_tensor(pe, 0)
                    barrier(pe, "first norm")
                proj_tensor(pe, l)
                barrier(pe, f"in-projection {l}")
                mixer_tensor(pe, l)
                barrier(pe, f"mixer {l}")
                gate_tensor(pe, l, 0)
                barrier(pe, f"mixer gate {l}")
                pass_tensor(pe, 2 * l + 1)
                barrier(pe, f"mixer output {l}")
                mlp_tensor(pe, l)
                barrier(pe, f"mlp {l}")
                gate_tensor(pe, l, 1)
                barrier(pe, f"mlp gate {l}")
                pass_tensor(pe, 2 * l + 2)
                barrier(pe, f"mlp output {l}")

        @block.vector
        def _(dve):
            chain = Chain(dve, dchain_sem)
            silu_vector(dve, chain)
            barrier(dve, "constants")
            ada_vector(dve, chain)
            barrier(dve, "adaln 0")
            for l in range(LAYERS):
                if l == 0:
                    pass_vector(dve, chain, 0)
                    barrier(dve, "first norm")
                if l == 0:
                    proj_vector(dve, chain)
                barrier(dve, f"in-projection {l}")
                mixer_vector(dve, chain, l)
                barrier(dve, f"mixer {l}")
                gate_vector(dve, l, 0)
                barrier(dve, f"mixer gate {l}")
                pass_vector(dve, chain, 2 * l + 1)
                barrier(dve, f"mixer output {l}")
                mlp_vector(dve, l)
                barrier(dve, f"mlp {l}")
                gate_vector(dve, l, 1)
                barrier(dve, f"mlp gate {l}")
                pass_vector(dve, chain, 2 * l + 2)
                barrier(dve, f"mlp output {l}")


def rope_tables():
    n = SAMPLE_TILES * P
    row, col = np.arange(n) // 64, np.arange(n) % 64
    inv = np.power(np.float32(10000.0), -np.arange(16, dtype=np.float32) / np.float32(16)).astype(np.float32)
    ang = np.concatenate([row[:, None].astype(np.float32) * inv, col[:, None].astype(np.float32) * inv], axis=-1)
    cs = np.zeros((TILES * P, 2, 32), np.float32)
    cs[:, 0] = 1
    cs[:n, 0], cs[:n, 1] = np.cos(ang), np.sin(ang)
    return cs.reshape(TILES, P, 2, 32)


def mixer_arrays(i, cols):
    a = {}
    a["rope"] = rope_tables()
    a["qk_gain"] = np.concatenate([np.tile(i["attn_q_norm"][0], HEADS), np.tile(i["attn_k_norm"][0], KV)]).reshape(1, 10 * HD)
    a["cache_kT"] = i["cache_attn_k"][0, 0].transpose(0, 2, 1).reshape(P, PAST)
    a["cache_v"] = i["cache_attn_v"][0, 0].transpose(1, 0, 2).reshape(2, P, P).transpose(1, 0, 2)
    rows36 = np.zeros((36, 2), np.float32)
    for d in range(2):
        rows36[32 * d:32 * d + MH, 0] = i["mlstm_i_bias"][0, d]
        rows36[32 * d:32 * d + MH, 1] = i["mlstm_f_bias"][0, d]
    a["gate_bias"] = rows36
    a["m_start"] = i["state_mlstm_m"][0, 0].reshape(2, MH, 1)
    a["C_start"] = np.concatenate([i["state_mlstm_C"][0, 0], i["state_mlstm_n"][0, 0][..., None]], axis=-1).reshape(8, MD, MD + 1).transpose(1, 0, 2)
    a["mlstm_gain"] = i["mlstm_norm"][0].reshape(1, 512)
    wr, wi = i["lru_w_r"][0], i["lru_w_i"][0]
    mat = np.zeros((4, P, 4, P), np.float32)
    for t in range(4):
        for b in range(2):
            for d in range(2):
                for g, w in enumerate((wr, wi)):
                    mat[t, 64 * b:64 * b + 64, 2 * d + g, 64 * b:64 * b + 64] = w[d, 2 * t + b]
    a["lru_mat"] = mat
    a["lru_bias"] = cols(np.stack([i["lru_b_r"][0], i["lru_b_i"][0]], axis=1)).reshape(P, 4, 4).transpose(0, 2, 1)
    a["lru_lam"], a["lru_h0"] = cols(i["lru_lambda"][0]), cols(i["state_lru_h"][0, 0])
    a["lru_conv"] = cols(np.concatenate([i["lru_conv_w"][0], i["lru_conv_b"]])).transpose(0, 2, 1)
    w = np.zeros((32, 4, P), np.float32)
    for d in range(2):
        w[RANK * d:RANK * (d + 1), 2 * d:2 * d + 2] = i["gla_w_lr"][0, d].reshape(RANK, 2, P)
    a["gla_w"], a["gla_b"] = w, cols(i["gla_b_lr"][0]).reshape(P, 4)
    a["gla_gain"] = i["gla_norm"][0].reshape(1, 512)
    a["gla_S"] = i["state_gla_S"][0, 0].reshape(2, 2, 2, GK, GV).transpose(2, 3, 0, 1, 4).reshape(2, GK, 4, GV)
    t = np.arange(P)
    same = [(t[:, None] // b == t // b) & (t[:, None] * 2 // b != t * 2 // b) for b in (P >> n for n in range(7))]
    a["level_mask"] = np.stack(same, axis=1).astype(np.int32)
    return a


MIXER_OUTS = {"new_h": (P, 2, 4), "new_k": (P, P), "new_v": (P, P), "new_m": (2, MH, 1), "new_C": (P, 8, MD + 1), "new_S": (2, GK, 4, GV)}


def column_order():
    sizes = [HEADS * HD, KV * HD, KV * HD, 512, 512, 512, 512, 8, 8]
    at = np.cumsum([0] + sizes)
    q = np.concatenate([np.arange(h * HD, (h + 1) * HD) for j in range(4) for h in (j, j + 4)])
    part = [np.arange(at[i], at[i + 1]) for i in range(9)]
    return np.concatenate([q, part[1], part[2], part[7], part[8], part[3], part[4], part[5], part[6]])


def host_arrays(i):
    c = np.ascontiguousarray
    both = lambda a: np.stack([a, a], axis=-1)
    cols = lambda a: np.moveaxis(a.reshape(a.shape[:-1] + (-1, P)), -1, 0)
    a = {}
    a["x_all"] = np.concatenate([i["x_sample"].reshape(SAMPLE_TILES, P, D), i["x_prompt"].reshape(1, P, D)])
    a["c_cols"] = np.stack([cols(i["c"][0]), cols(i["c_ctx"])], axis=-1)
    a["ada_w"], a["ada_b"] = i["ada_w"], both(cols(i["ada_b"]))
    a["gains"] = both(cols(np.stack([i[n] for n in ("norm_mix_pre", "norm_mix_post", "norm_ffn_pre", "norm_ffn_post")], axis=1)))
    a["w_in_even"] = i["w_in_even"][0][:, column_order()]
    a["w_in_odd"] = i["w_in_odd"][0]
    a["w_out"], a["ffn_w1"], a["ffn_w2"] = i["w_out"], i["ffn_w1"], i["ffn_w2"]
    a.update(mixer_arrays(i, cols))
    return {k: c(v) for k, v in a.items()}


def kernel(**inputs):
    import concourse.bacc as bacc
    from concourse import mybir as mb
    from concourse.bass_utils import run_bass_kernel_spmd

    arrays = host_arrays({n: np.asarray(a) for n, a in inputs.items()})
    nc = bacc.Bacc("TRN2", target_bir_lowering=False, num_devices=1)
    args = {n: nc.dram_tensor(n, a.shape, mb.dt.from_np(a.dtype), kind="ExternalInput").ap() for n, a in arrays.items()}
    for n, shape in dict(MIXER_OUTS, y_all=(TILES, P, D)).items():
        args[n] = nc.dram_tensor(n, shape, F32, kind="ExternalOutput").ap()
    trunk(nc, args)
    r = run_bass_kernel_spmd(nc, [arrays], core_ids=[0]).results[0]
    c = np.ascontiguousarray
    heads = lambda a: c(a.reshape(P, KV, HD).transpose(1, 0, 2)).reshape(1, 1, KV, P, HD)
    C = r["new_C"]
    return (c(r["y_all"][SAMPLE_TILES]).reshape(1, P, D), c(r["y_all"][:SAMPLE_TILES]).reshape(1, SAMPLE_TILES * P, D), heads(r["new_k"]), heads(r["new_v"]),
            c(C[:, :, :MD].transpose(1, 0, 2)).reshape(1, 1, 2, MH, MD, MD), c(C[:, :, MD].T).reshape(1, 1, 2, MH, MD), r["new_m"].reshape(1, 1, 2, MH),
            c(r["new_h"].transpose(1, 2, 0)).reshape(1, 1, 2, LW), c(r["new_S"].reshape(2, GK, 2, 2, GV).transpose(2, 3, 0, 1, 4)).reshape(1, 1, 2, GH, GK, GV))
```
